# Optimizing a Trainium2 kernel written in Bass

```python
import math
import jax, jax.numpy as jnp
from jax import lax
import numpy as np

D_MODEL = 1024
BATCH = 1
SEQ = 2048
DEPTH = 1

HEAD_DIM = 64
SWA_Q_HEADS = 8
SWA_KV_HEADS = 2
SB_HEADS = 8
WINDOW = 128
BLOCK = 128
ROPE_THETA = 10000.0
EPS = 1e-6
SWA_WIDTH = SWA_Q_HEADS * HEAD_DIM
SWA_KV_WIDTH = SWA_KV_HEADS * HEAD_DIM
SB_WIDTH = SB_HEADS * HEAD_DIM
MIX_WIDTH = SWA_WIDTH + SB_WIDTH
SPLITS = (SWA_WIDTH, SWA_KV_WIDTH, SWA_KV_WIDTH, SWA_WIDTH, SB_WIDTH, SB_WIDTH, SB_WIDTH, SB_WIDTH)
IN_WIDTH = sum(SPLITS)

kernel_name = "hybrid_swa_sink_stickbreaking_heads"

def rmsnorm(x, g):
    xf = x.astype(jnp.float32)
    y = xf * lax.rsqrt(jnp.mean(xf * xf, axis=-1, keepdims=True) + EPS)
    return (y * g.astype(jnp.float32)).astype(x.dtype)

def rope(x, positions):
    half = x.shape[-1] // 2
    inv_freq = ROPE_THETA ** (-jnp.arange(half, dtype=jnp.float32) * 2.0 / x.shape[-1])
    ang = positions.astype(jnp.float32)[..., None] * inv_freq
    cos = jnp.cos(ang)[:, :, None, :]
    sin = jnp.sin(ang)[:, :, None, :]
    xf = x.astype(jnp.float32)
    x1, x2 = xf[..., :half], xf[..., half:]
    out = jnp.concatenate([x1 * cos - x2 * sin, x2 * cos + x1 * sin], axis=-1)
    return out.astype(x.dtype)

def swa_sink_attention(q, k, v, sinks):
    B, S, Hq, d = q.shape
    Hkv = k.shape[2]
    G = Hq // Hkv
    nb = S // BLOCK
    scale = 1.0 / math.sqrt(d)
    qb = q.reshape(B, nb, BLOCK, Hkv, G, d)
    kb = k.reshape(B, nb, BLOCK, Hkv, d)
    vb = v.reshape(B, nb, BLOCK, Hkv, d)
    kprev = jnp.concatenate([jnp.zeros_like(kb[:, :1]), kb[:, :-1]], axis=1)
    vprev = jnp.concatenate([jnp.zeros_like(vb[:, :1]), vb[:, :-1]], axis=1)
    kw = jnp.concatenate([kprev, kb], axis=2)
    vw = jnp.concatenate([vprev, vb], axis=2)
    scores = jnp.einsum('bnqhgd,bnkhd->bnhgqk', qb, kw).astype(jnp.float32) * scale
    q_idx = jnp.arange(nb)[:, None] * BLOCK + jnp.arange(BLOCK)[None, :]
    k_idx = jnp.arange(nb)[:, None] * BLOCK - BLOCK + jnp.arange(2 * BLOCK)[None, :]
    diff = q_idx[:, :, None] - k_idx[:, None, :]
    mask = (diff >= 0) & (diff < WINDOW) & (k_idx[:, None, :] >= 0)
    scores = jnp.where(mask[None, :, None, None], scores, -jnp.inf)
    sink = sinks.astype(jnp.float32).reshape(Hkv, G)[None, None, :, :, None, None]
    m = jnp.maximum(jnp.max(scores, axis=-1, keepdims=True), sink)
    p = jnp.exp(scores - m)
    probs = p / (jnp.sum(p, axis=-1, keepdims=True) + jnp.exp(sink - m))
    out = jnp.einsum('bnhgqk,bnkhd->bnqhgd', probs.astype(v.dtype), vw)
    return out.reshape(B, S, Hq * d)

def stick_breaking_attention(q, k, v):
    B, S, H, d = q.shape
    nb = S // BLOCK
    scale = 1.0 / math.sqrt(d)
    outs = []
    for i in range(nb):
        t0 = i * BLOCK
        L = t0 + BLOCK
        qi = q[:, t0:L]
        kp = k[:, :L]
        vp = v[:, :L]
        z = jnp.einsum('bqhd,bkhd->bhqk', qi, kp).astype(jnp.float32) * scale
        t_idx = t0 + jnp.arange(BLOCK)[:, None]
        s_idx = jnp.arange(L)[None, :]
        causal = s_idx < t_idx
        log_fail = jnp.where(causal, jax.nn.log_sigmoid(-z), 0.0)
        after = lax.cumsum(log_fail, axis=3, reverse=True) - log_fail
        w = jnp.where(causal, jnp.exp(jax.nn.log_sigmoid(z) + after), 0.0)
        outs.append(jnp.einsum('bhqk,bkhd->bqhd', w.astype(v.dtype), vp))
    out = jnp.concatenate(outs, axis=1)
    return out.reshape(B, S, H * d)

def setup_inputs(seed: int = 0) -> dict:
    key = jax.random.key(seed)
    ks = jax.random.split(key, 8)
    x = jax.random.normal(ks[0], (BATCH, SEQ, D_MODEL), jnp.float32)
    positions = jnp.broadcast_to(jnp.arange(SEQ, dtype=jnp.int32)[None, :], (BATCH, SEQ)).astype(jnp.int32)
    norm_gain = 1.0 + 0.02 * jax.random.normal(ks[1], (DEPTH, D_MODEL), jnp.float32)
    w_in = jax.random.normal(ks[2], (DEPTH, D_MODEL, IN_WIDTH), jnp.float32) * D_MODEL ** -0.5
    q_norm_gain = 1.0 + 0.02 * jax.random.normal(ks[3], (DEPTH, HEAD_DIM), jnp.float32)
    k_norm_gain = 1.0 + 0.02 * jax.random.normal(ks[4], (DEPTH, HEAD_DIM), jnp.float32)
    sinks = 0.5 * jax.random.normal(ks[5], (DEPTH, SWA_Q_HEADS), jnp.float32)
    w_out = jax.random.normal(ks[6], (DEPTH, MIX_WIDTH, D_MODEL), jnp.float32) * MIX_WIDTH ** -0.5
    return {"x": x, "positions": positions, "norm_gain": norm_gain, "w_in": w_in,
            "q_norm_gain": q_norm_gain, "k_norm_gain": k_norm_gain, "sinks": sinks, "w_out": w_out}

def reference(x, positions, norm_gain, w_in, q_norm_gain, k_norm_gain, sinks, w_out):
    B, S, _ = x.shape
    split_points = list(np.cumsum(SPLITS)[:-1])
    for l in range(DEPTH):
        h = rmsnorm(x, norm_gain[l])
        proj = jnp.einsum('bsd,de->bse', h, w_in[l])
        qa, ka, va, ga, qb, kb, vb, gb = jnp.split(proj, split_points, axis=-1)
        qa = rope(rmsnorm(qa.reshape(B, S, SWA_Q_HEADS, HEAD_DIM), q_norm_gain[l]), positions)
        ka = rope(rmsnorm(ka.reshape(B, S, SWA_KV_HEADS, HEAD_DIM), k_norm_gain[l]), positions)
        va = va.reshape(B, S, SWA_KV_HEADS, HEAD_DIM)
        ya = swa_sink_attention(qa, ka, va, sinks[l]) * jax.nn.silu(ga)
        qb = qb.reshape(B, S, SB_HEADS, HEAD_DIM)
        kb = kb.reshape(B, S, SB_HEADS, HEAD_DIM)
        vb = vb.reshape(B, S, SB_HEADS, HEAD_DIM)
        yb = stick_breaking_attention(qb, kb, vb) * jax.nn.silu(gb)
        y = jnp.concatenate([ya, yb], axis=-1)
        x = x + jnp.einsum('bse,ed->bsd', y, w_out[l])
    return x


_drawn_inputs = setup_inputs


def setup_inputs(seed=0):
    import zlib

    import numpy as np

    out = dict(_drawn_inputs(seed))
    spreads = {}
    factors = {'norm_gain': 6.132, 'q_norm_gain': 8.0, 'k_norm_gain': 8.0, 'sinks': 200.0}
    for name, (base, spread) in spreads.items():
        noise = np.random.default_rng([zlib.crc32(name.encode()), seed]).standard_normal(out[name].shape)
        drawn = base * np.exp(spread * noise) if base else spread * noise
        out[name] = __import__('jax').numpy.asarray(drawn.astype(out[name].dtype))
    for name, factor in factors.items():
        out[name] = (out[name] * factor).astype(out[name].dtype)
    return out
```

```python
from contextlib import ExitStack

import numpy as np
from concourse import mybir

F32 = mybir.dt.float32
F32R = mybir.dt.float32r
BF16 = mybir.dt.bfloat16
I32 = mybir.dt.int32
ALU = mybir.AluOpType
ACT = mybir.ActivationFunctionType
AX = mybir.AxisListType

P = 128
SEQ, D_MODEL = 2048, 1024
HD = 64
HALF = HD // 2
KB = D_MODEL // P
GRP = 512
NG = SEQ // GRP
NT = SEQ // P
TPG = GRP // P
SWA_Q, SWA_KV, SB_H = 8, 2, 8
GQ = SWA_Q // SWA_KV
RAW_BLOCKS = 10
GATE_BLOCK = 6
SPLIT_BLOCKS = 16
QK = SWA_Q + SWA_KV
EPS = 1e-6
SCALE = HD ** -0.5
MASKED = -1e30
THETA = 10000.0
PI = float(np.float32(3.1415925))
TWO_PI_PARTS = (6.25, 0.033203125, -1.7881393432617188e-05, 2 * np.pi - 6.25 - 0.033203125 + 1.7881393432617188e-05)
ROUND = float(1.5 * 2 ** 23)


def view(buf, at, shape):
    n = int(np.prod(shape))
    v = buf[:, at:at + n]
    if len(shape) == 2:
        v = v.rearrange("p (a b) -> p a b", a=shape[0])
    return v


def spread(ap, n, where):
    shape = list(ap.shape)
    shape.insert(where, n)
    return ap.unsqueeze(where).broadcast_to(shape)


class Chain:

    def __init__(self, eng, sem):
        self.eng, self.sem, self.n, self.turn = eng, sem, 0, 0

    def link(self, ins):
        ins.then_inc(self.sem, 1)
        self.n += 1
        self.eng.wait_ge(self.sem, self.turn + self.n)

    def enter(self, i, per_turn):
        self.turn, self.base, self.per_turn = i * per_turn, self.n, per_turn

    def leave(self, turns):
        assert self.n - self.base == self.per_turn, (self.n - self.base, self.per_turn)
        self.turn, self.n = 0, self.base + turns * self.per_turn


def newton_rsqrt(dve, chain, y, ms, tmp):
    chain.link(dve.tensor_tensor(tmp, y, y, ALU.mult))
    chain.link(dve.tensor_tensor(tmp, tmp, ms, ALU.mult))
    chain.link(dve.tensor_scalar(tmp, tmp, -0.5, 1.5, ALU.mult, ALU.add))
    chain.link(dve.tensor_tensor(y, y, tmp, ALU.mult))


def project(nc, c, t):
    sb = lambda n, s, d=F32: c.enter_context(nc.sbuf_tensor(n, s, d))
    sem = lambda n: c.enter_context(nc.semaphore(n))
    ht_hi, ht_lo = sb("ht_hi", [P, KB, SEQ], F32R), sb("ht_lo", [P, KB, SEQ], F32R)
    w_hi, w_lo = sb("w_hi", [P, 2, KB, P], F32R), sb("w_lo", [P, 2, KB, P], F32R)
    w_raw = sb("w_raw", [P, 2, KB // 2, P])
    arena = sb("arena", [P, 5248])
    x_in = view(arena, 0, (TPG, D_MODEL))
    qkv_t = view(arena, 0, (6, P))
    qkv = view(arena, 768, (QK + SWA_KV, HD))
    qk, v_raw = qkv[:, 0:QK, :], qkv[:, QK:, :]
    rot = view(arena, 1536, (2, QK * HALF))
    rot1, rot2 = (rot[:, n, :].rearrange("p (h d) -> p h d", h=QK) for n in range(2))
    probs = view(arena, 2176, (GQ, 2 * P))
    y_sum = view(arena, 2176, (GQ, P))[0:HD]
    gate_t = view(arena, 3200, (SWA_Q, P))[0:HD]
    stage_raw = view(arena, 2176, (NG, GRP))
    rope_tmp = [view(arena, 512 * n, (NT, HALF)) for n in range(3)]
    cos, sin = view(arena, 4224, (NT, HALF)), view(arena, 4736, (NT, HALF))
    stage_hi, stage_lo = sb("stage_hi", [P, 2, GRP], F32R), sb("stage_lo", [P, 2, GRP], F32R)
    qk_split = sb("qk_split", [P, QK + SWA_KV, P], F32R)
    q_t = sb("q_t", [P, SWA_Q, P], F32R)
    k_t = sb("k_t", [P, 2, SWA_KV, 2, P], F32R)
    v_s = sb("v_s", [P, 2, SWA_KV, P], F32R)
    p_hi, p_lo = sb("p_hi", [P, 2 * GQ * P], F32R), sb("p_lo", [P, 2 * GQ * P], F32R)
    y_hi, y_lo = p_hi[0:HD, 0:GQ * P], p_lo[0:HD, 0:GQ * P]
    ident, ident_bf = sb("ident", [P, P]), sb("ident_bf", [P, P], BF16)
    mask_even = sb("mask_even", [P, 2, 2 * P], BF16)
    mask_odd = sb("mask_odd", [P, 2 * P], BF16)
    gain = sb("gain", [P, KB])
    qk_gain = sb("qk_gain", [P, 2, HD])
    sink = sb("sink", [P, SWA_Q])
    inv_freq = sb("inv_freq", [P, HALF])
    pos_i, pos = sb("pos_i", [P, NT], I32), sb("pos", [P, NT])
    power = sb("power", [P, QK])
    ssq, ms, rs, rtmp = (sb(n, [P, QK]) for n in ("ssq", "ms", "rs", "rtmp"))
    top, neg_top, sink_e, den = (sb(n, [P, GQ]) for n in ("top", "neg_top", "sink_e", "den"))
    bank = [c.enter_context(nc.psum_tensor(f"bank{n}", [P, GRP], F32)) for n in range(4)]
    X = c.enter_context(nc.psum_tensor("X", [P, 2 * GRP], F32))
    Y = c.enter_context(nc.psum_tensor("Y", [P, 2 * GRP], F32))
    xbank = [b[:, :] for b in bank] + [X[:, 0:GRP], X[:, GRP:], Y[:, 0:GRP], Y[:, GRP:]]

    x_loaded = [sem(f"x_loaded{a}") for a in range(TPG)]
    consts_in, pos_in = sem("consts_in"), sem("pos_in")
    ssq_done, ms_done, pow_done, x_scaled = sem("ssq_done"), sem("ms_done"), sem("pow_done"), sem("x_scaled")
    x_used = sem("x_used")
    xt_done, ht_hi_done, ht_lo_done = sem("xt_done"), sem("ht_hi_done"), sem("ht_lo_done")
    pool_chain, dve_chain, act_chain = sem("pool_chain"), sem("dve_chain"), sem("act_chain")
    consts_made = sem("consts_made")
    w_loaded = [sem(f"w_loaded{h}") for h in range(2)]
    w_hi_done, w_split = sem("w_hi_done"), sem("w_split")
    sigmoid_done = sem("sigmoid_done")
    proj_done, raw_done, hi_done, split_done = sem("proj_done"), sem("raw_done"), sem("hi_done"), sem("split_done")
    raw_out = [sem(f"raw_out{g}") for g in range(NG)]
    split_out = [sem(f"split_out{s}") for s in range(2)]
    angles_done, rope_done = sem("angles_done"), sem("rope_done")
    qkv_in, gate_in = sem("qkv_in"), sem("gate_in")
    tin_done, qk_out, v_hi_done, v_done = sem("tin_done"), sem("qk_out"), sem("v_hi_done"), sem("v_done")
    rot_done, qs_hi_done, qs_lo_done, qs_done = sem("rot_done"), sem("qs_hi_done"), sem("qs_lo_done"), sem("qs_done")
    tq_done, q_ready, tk_done, k_ready = sem("tq_done"), sem("q_ready"), sem("tk_done"), sem("k_ready")
    sc_done, top_done, exp_done, p_done = sem("sc_done"), sem("top_done"), sem("exp_done"), sem("p_done")
    pt_done, p_hi_done, p_split = sem("pt_done"), sem("p_hi_done"), sem("p_split")
    pv_done, yv_done, y_read, y_gated = sem("pv_done"), sem("yv_done"), sem("y_read"), sem("y_gated")
    y_hi_done, y_done, y_out = sem("y_hi_done"), sem("y_done"), sem("y_out")
    w_seen, y_seen = sem("w_seen"), sem("y_seen")
    block = c.enter_context(nc.Block())

    w_view = t["w_in"].rearrange("l (k p) n -> p (l k) n", p=P)
    raw_view = t["raw"].rearrange("(b p) t -> p b t", p=P)
    gate_view = t["raw"][6 * P:RAW_BLOCKS * P, :].rearrange("(h d) t -> d h t", d=HD)
    y_views = [t[n][0:SWA_Q * HD, :].rearrange("(h d) t -> d h t", d=HD) for n in ("y_hi", "y_lo")]

    @block.sync
    def _(sp):
        from concourse.bass import ds

        def load_x(a, tile):
            sp.dma_start(x_in[:, a, :], t["x"][0, ds(tile * P, P), :]).then_inc(x_loaded[a], 16)

        def load_w(b):
            for h in range(2):
                sp.dma_start(w_raw[:, h], w_view[:, 4 * h:4 * h + 4, ds(b * P, P)]).then_inc(w_loaded[h], 16)

        def prefetch_w(b):
            for h in range(2):
                sp.wait_ge(w_split, 2 * b + h + 1)
                sp.dma_start(w_raw[:, h], w_view[:, 4 * h:4 * h + 4, ds((b + 1) * P, P)]).then_inc(w_loaded[h], 16)

        for a in range(TPG):
            load_x(a, a)
        with nc.allow_non_contiguous_dma(reason="small columns of constants"):
            sp.dma_start(gain[:, :], t["norm_gain"].rearrange("l (k p) -> p (l k)", p=P)).then_inc(consts_in, 16)
            sp.dma_start(pos_i[:, :], t["positions"].rearrange("b (n p) -> p (b n)", p=P)).then_inc(pos_in, 16)
        sp.dma_start(qk_gain[:, 0, :], t["q_norm_gain"].broadcast_to([P, HD])).then_inc(consts_in, 16)
        sp.dma_start(qk_gain[:, 1, :], t["k_norm_gain"].broadcast_to([P, HD])).then_inc(consts_in, 16)
        sp.dma_start(sink[:, :], t["sinks"].broadcast_to([P, SWA_Q])).then_inc(consts_in, 16)
        load_w(0)
        with sp.Fori(1, NG) as g:
            for a in range(TPG):
                sp.wait_ge(*((x_used, g) if a < 2 else (xt_done, KB * g)))
                load_x(a, TPG * g + a)

        def raw_block(b):
            prefetch_w(b)
            for g in range(NG):
                sp.wait_ge(raw_done, NG + NG * b + g + 1)
                sp.dma_start(t["raw"][ds(b * P, P), g * GRP:(g + 1) * GRP],
                             stage_raw[:, g, :]).then_inc(raw_out[g], 16)

        with sp.Fori(0, RAW_BLOCKS // 2 - 1) as i:
            for p in range(2):
                raw_block(2 * i + p)

        def load_qkv(tile, n):
            sp.wait_ge(tin_done, n)
            sp.dma_start(qkv_t, raw_view[:, 0:6, ds(tile * P, P)]).then_inc(qkv_in, 16)

        def store_y(tile, half):
            n = 2 * tile + half
            sp.wait_ge(y_done, n + 1)
            sp.sem_inc(y_seen, 1)
            for y, v in zip((y_hi, y_lo), y_views):
                sp.dma_start(v[:, GQ * half:GQ * half + GQ, ds(tile * P, P)],
                             y.bitcast(F32).rearrange("d (h t) -> d h t", h=GQ)).then_inc(y_out, 16)

        def split_block(tile, more):
            nxt = sp.snap((tile + 1) % NT) if more else 0
            if more:
                prefetch_w(tile + RAW_BLOCKS)
            sp.wait_ge(y_gated, 2 * tile)
            sp.dma_start(gate_t, gate_view[:, :, ds(tile * P, P)]).then_inc(gate_in, 16)
            load_qkv(nxt, tile + 1)
            for g in range(NG):
                sp.wait_ge(split_done, NG + NG * tile + g + 1)
                for st, d in ((stage_hi, "hi"), (stage_lo, "lo")):
                    sp.dma_start(t[d][ds(tile * P, P), g * GRP:(g + 1) * GRP],
                                 st[:, g % 2, :].bitcast(F32)).then_inc(split_out[g % 2], 16)
                if g >= 2:
                    store_y(tile, g - 2)

        for g in range(NG):
            sp.wait_ge(raw_out[g], 16 * (RAW_BLOCKS - 2))
        sp.wait_ge(angles_done, 1)
        load_qkv(0, 0)
        raw_block(RAW_BLOCKS - 2)
        raw_block(RAW_BLOCKS - 1)
        for g in range(NG):
            sp.wait_ge(raw_out[g], 16 * RAW_BLOCKS)
        with sp.Fori(0, NT // 2 - 1) as i:
            for p in range(2):
                split_block(2 * i + p, True)
        split_block(NT - 2, True)
        split_block(NT - 1, False)
        sp.wait_ge(y_out, 16 * 2 * 2 * NT)
        for s in range(2):
            sp.wait_ge(split_out[s], 16 * 2 * 2 * NT)

    @block.gpsimd
    def _(pool):
        chain = Chain(pool, pool_chain)

        pool.memset(power[:, :], -0.5).then_inc(consts_made, 1)
        for n in range(HALF):
            ins = pool.memset(inv_freq[:, n:n + 1], float(np.float32(THETA) ** np.float32(-n * 2.0 / HD)))
        ins.then_inc(consts_made, 1)
        chain.link(pool.memset(ident[:, :], 0.0))
        chain.link(pool.affine_select(out=ident[:, :], in_=ident[:, :], compare_op=ALU.not_equal, fill=1.0,
                                      base=0, pattern=[[-1, P]], channel_multiplier=1))
        pool.tensor_copy(ident_bf[:, :], ident[:, :]).then_inc(consts_made, 1)

        with pool.Fori(0, NG) as g:
            pool.wait_ge(ms_done, g + 1)
            pool.tensor_tensor(rs[:, 0:TPG], ms[:, 0:TPG], power[:, 0:TPG], ALU.pow).then_inc(pow_done, 1)

        chain.link(pool.memset(mask_even[:, :, :], 0.0))
        chain.link(pool.memset(mask_odd[:, :], 0.0))
        own = dict(compare_op=ALU.is_ge, fill=MASKED, base=0, pattern=[[-1, P]], channel_multiplier=1)
        before = dict(compare_op=ALU.is_gt, fill=MASKED, base=0, pattern=[[1, P]], channel_multiplier=-1)
        for n in range(2):
            chain.link(pool.affine_select(out=mask_even[:, n, 0:P], in_=mask_even[:, n, 0:P], **own))
        chain.link(pool.memset(mask_even[:, 0, P:], MASKED))
        chain.link(pool.affine_select(out=mask_even[:, 1, P:], in_=mask_even[:, 1, P:], **before))
        chain.link(pool.affine_select(out=mask_odd[:, 0:P], in_=mask_odd[:, 0:P], **before))
        pool.affine_select(out=mask_odd[:, P:], in_=mask_odd[:, P:], **own).then_inc(consts_made, 1)
        pool.memset(k_t[:, :, :, 1, :].bitcast(F32), 0.0).then_inc(consts_made, 1)
        pool.memset(v_s[:, 1].bitcast(F32), 0.0).then_inc(consts_made, 1)

        def split_w(b, p, free):
            if free is not None:
                pool.wait_ge(proj_done, free)
            for h in range(2):
                at = slice(4 * h, 4 * h + 4)
                pool.wait_ge(w_loaded[h], 16 * (b + 1))
                pool.sem_inc(w_seen, 1)
                pool.tensor_copy(w_hi[:, p, at], w_raw[:, h]).then_inc(w_hi_done, 1)
                pool.wait_ge(w_hi_done, 2 * b + h + 1)
                pool.tensor_tensor(w_lo[:, p, at], w_raw[:, h], w_hi[:, p, at].bitcast(F32),
                                   ALU.subtract).then_inc(w_split, 1)

        split_w(0, 0, None)
        split_w(1, 1, None)

        with pool.Fori(1, RAW_BLOCKS // 2) as i:
            for p in range(2):
                split_w(2 * i + p, p, NG * (2 * i + p - 1))

        def qk_power(n):
            pool.wait_ge(ms_done, NG + n + 1)
            pool.tensor_tensor(rs[:, :], ms[:, :], power[:, :], ALU.pow).then_inc(pow_done, 1)

        qk_power(0)
        with pool.Fori(RAW_BLOCKS // 2, (RAW_BLOCKS + SPLIT_BLOCKS) // 2) as i:
            for p in range(2):
                split_w(2 * i + p, p, NG * (2 * i + p - 1))
                qk_power(2 * i + p - RAW_BLOCKS + 1)

    @block.tensor
    def _(pe):
        from concourse.bass import ds
        mm = pe.matmul
        pe.wait_ge(consts_made, 3)
        with pe.Fori(0, NG) as g:
            pe.wait_ge(ht_lo_done, KB * g)
            for pair in range(2):
                pe.wait_ge(x_scaled, TPG * g + 2 * pair + 2)
                for k in range(KB):
                    for a in (2 * pair, 2 * pair + 1):
                        ins = pe.transpose(xbank[k][:, a * P:(a + 1) * P], x_in[:, a, k * P:(k + 1) * P], ident[:, :])
                    if pair:
                        ins.then_inc(xt_done, 1)
                if not pair:
                    ins.then_inc(x_used, 1)
        pe.wait_ge(ht_lo_done, KB * NG)
        pe.wait_ge(consts_made, 6)

        def project_half(b, p, g, half):
            passes = [(w, h, k) for w, h in ((w_hi, ht_hi), (w_hi, ht_lo), (w_lo, ht_hi)) for k in range(KB)]
            for n in range(12 * half, 12 * half + 12):
                w, h, k = passes[n]
                ins = mm(bank[g][:, :], w[:, p, k, :], h[:, k, g * GRP:(g + 1) * GRP], start=n == 0, stop=n == 23)
            if half:
                ins.then_inc(proj_done, 1)

        def tokens_out(n):
            pe.wait_ge(qkv_in, 16 * (n + 1))
            pe.wait_ge(k_ready, n)
            for j in range(6):
                ins = pe.transpose(X[:, j * P:(j + 1) * P], qkv_t[:, j, :], ident[:, :])
            ins.then_inc(tin_done, 1)

        def q_columns(n):
            pe.wait_ge(qk_out, n + 1)
            pe.wait_ge(qs_done, n + 1)
            for j in range(SWA_Q):
                ins = pe.transpose(X[:, j * P:(j + 1) * P], qk_split[:, j, :].bitcast(F32), ident[:, :])
            ins.then_inc(tq_done, 1)

        def k_columns(n):
            pe.wait_ge(q_ready, n + 1)
            for j in range(2 * SWA_KV):
                ins = pe.transpose(X[:, j * P:(j + 1) * P], qk_split[:, SWA_Q + j, :].bitcast(F32), ident[:, :])
            ins.then_inc(tk_done, 1)

        def scores(n, half, mask):
            pe.wait_ge(k_ready, n + 1)
            pe.wait_ge(y_read, 2 * n + half)
            for j in range(GQ):
                out = Y[:, j * 2 * P:(j + 1) * 2 * P]
                mm(out, ident_bf[:, :], mask, start=True, stop=False)
                for s in range(2):
                    ins = mm(out, q_t[:, GQ * half + j, :], k_t[:, s, half, :, :].rearrange("p a b -> p (a b)"),
                             start=False, stop=s == 1)
            ins.then_inc(sc_done, 1)

        def probs_t(n, half):
            pe.wait_ge(p_done, 2 * n + half + 1)
            for s in range(2):
                for j in range(GQ):
                    at = (s * GQ + j) * P
                    ins = pe.transpose(Y[:, at:at + P], probs[:, j, s * P:(s + 1) * P], ident[:, :])
            ins.then_inc(pt_done, 1)

        def values(n, half):
            pe.wait_ge(v_done, n + 1)
            pe.wait_ge(p_split, 2 * n + half + 1)
            for s in range(2):
                for m, part in enumerate((p_hi, p_lo)):
                    ins = mm(Y[:, 0:GRP], v_s[:, s, half, :], part[:, s * GRP:(s + 1) * GRP],
                             start=s == 0 and m == 0, stop=s == 1 and m == 1)
            ins.then_inc(pv_done, 1)

        with pe.Fori(0, RAW_BLOCKS // 2 - 1) as i:
            for p in range(2):
                b = 2 * i + p
                pe.wait_ge(w_split, 2 * (b + 1))
                for g in range(NG):
                    pe.wait_ge(raw_done, NG * b + g + 1)
                    for half in range(2):
                        project_half(b, p, g, half)
        for p in range(2):
            b = RAW_BLOCKS - 2 + p
            pe.wait_ge(w_split, 2 * (b + 1))
            for g in range(NG):
                pe.wait_ge(raw_done, NG * b + g + 1)
                if (p, g) == (0, 0):
                    tokens_out(0)
                if (p, g) == (1, 0):
                    q_columns(0)
                if (p, g) == (1, 1):
                    k_columns(0)
                for half in range(2):
                    project_half(b, p, g, half)
        pe.wait_ge(raw_done, NG * (RAW_BLOCKS + 1))
        with pe.Fori(0, NT // 2) as i:
            for p in range(2):
                n = 2 * i + p
                b = n + RAW_BLOCKS
                if p:
                    mask = mask_odd[:, :]
                else:
                    mask = mask_even[:, :, :].rearrange("p a b -> p (a b)")[:, ds(((i + 7) // 8) * (2 * P), 2 * P)]
                pe.wait_ge(w_split, 2 * (b + 1))
                for g in range(NG):
                    pe.wait_ge(split_done, NG * n + g + 1)
                    if g == 0:
                        scores(n, 0, mask)
                        tokens_out(n + 1)
                    if g == 1:
                        probs_t(n, 0)
                    if g == 2:
                        scores(n, 1, mask)
                    if g == 3:
                        probs_t(n, 1)
                        k_columns(n + 1)
                    project_half(b, p, g, 0)
                    if g == 1:
                        values(n, 0)
                    if g == 2:
                        q_columns(n + 1)
                    if g == 3:
                        values(n, 1)
                    project_half(b, p, g, 1)

    @block.scalar
    def _(act):
        from concourse.bass import ds
        chain = Chain(act, act_chain)
        act.sem_inc(raw_done, NG)
        act.sem_inc(split_done, NG)
        act.wait_ge(consts_in, 64)
        with act.Fori(0, NG) as g:
            for a in range(TPG):
                act.wait_ge(x_loaded[a], 16 * (g + 1))
                act.wait_ge(ssq_done, TPG * g + a)
                act.activation(w_lo[:, 0].rearrange("p a b -> p (a b)"), x_in[:, a, :], ACT.Square,
                               accum_out=ssq[:, a:a + 1]).then_inc(ssq_done, 1)
            for k in range(KB):
                act.wait_ge(xt_done, KB * g + k + 1)
                act.activation(ht_hi[:, k, ds(g * GRP, GRP)], xbank[k], ACT.Copy,
                               scale=gain[:, k:k + 1]).then_inc(ht_hi_done, 1)

        def tile_in(n):
            act.wait_ge(v_done, n)
            act.wait_ge(tin_done, n + 1)
            act.activation(qkv.rearrange("p h d -> p (h d)"), X[:, 0:6 * P], ACT.Copy).then_inc(qk_out, 1)

        def v_high(n, p):
            act.wait_ge(pv_done, 2 * n)
            act.activation(v_s[:, p, :, 0:HD], v_raw, ACT.Copy).then_inc(v_hi_done, 1)

        def high_parts(n):
            act.wait_ge(rot_done, n + 1)
            act.wait_ge(tk_done, n)
            act.activation(qk_split[:, 0:QK, 0:HALF], rot1, ACT.Copy).then_inc(qs_hi_done, 1)
            act.activation(qk_split[:, 0:QK, HALF:HD], qk[:, :, HALF:HD], ACT.Copy).then_inc(qs_hi_done, 1)

        def swapped_k(n):
            act.wait_ge(qs_lo_done, n + 1)
            act.wait_ge(qs_hi_done, 2 * (n + 1))
            act.activation(qk_split[:, QK:, 0:HD], qk_split[:, SWA_Q:QK, HD:P].bitcast(F32), ACT.Copy)
            act.activation(qk_split[:, QK:, HD:P], qk_split[:, SWA_Q:QK, 0:HD].bitcast(F32),
                           ACT.Copy).then_inc(qs_done, 1)

        def q_out(n):
            act.wait_ge(tq_done, n + 1)
            act.wait_ge(sc_done, 2 * n)
            act.activation(q_t[:, :, :].rearrange("p a b -> p (a b)"), X[:, :], ACT.Copy).then_inc(q_ready, 1)

        def k_out(n, p):
            act.wait_ge(tk_done, n + 1)
            act.activation(k_t[:, :, :, p, :].rearrange("p a b c -> p (a b) c"),
                           X[:, 0:GRP].rearrange("p (a b) -> p a b", a=4), ACT.Copy).then_inc(k_ready, 1)

        def softmax(n, half):
            act.wait_ge(top_done, 2 * n + half + 1)
            for j in range(GQ):
                act.activation(probs[:, j, :], Y[:, j * 2 * P:(j + 1) * 2 * P], ACT.Exp, bias=neg_top[:, j:j + 1],
                               scale=SCALE, accum_out=den[:, j:j + 1])
            act.activation(sink_e[:, :], sink_e[:, :], ACT.Exp).then_inc(exp_done, 1)

        def p_high(n, half):
            act.wait_ge(pt_done, 2 * n + half + 1)
            act.wait_ge(y_out, 32 * (2 * n + half))
            act.activation(p_hi[:, :], Y[:, :], ACT.Copy).then_inc(p_hi_done, 1)

        def low_values(n, half):
            act.wait_ge(pv_done, 2 * n + half + 1)
            act.activation(y_sum, Y[HD:P, 0:GRP].rearrange("p (a b) -> p a b", a=GQ), ACT.Copy).then_inc(yv_done, 1)

        def y_high(n, half):
            act.wait_ge(y_gated, 2 * n + half + 1)
            act.activation(y_hi, y_sum.rearrange("p a b -> p (a b)"), ACT.Copy).then_inc(y_hi_done, 1)

        def raw_group(b, g):
            act.wait_ge(proj_done, NG * b + g + 1)
            act.wait_ge(raw_out[g], 16 * b)
            act.activation(stage_raw[:, g, :], bank[g][:, :], ACT.Copy).then_inc(raw_done, 1)

        def gate_group(b, g):
            act.wait_ge(proj_done, NG * b + g + 1)
            act.wait_ge(raw_out[g], 16 * b)
            act.activation(stage_raw[:, g, :], bank[g][:, :], ACT.Sigmoid).then_inc(sigmoid_done, 1)

        with act.Fori(0, GATE_BLOCK // 2) as i:
            for p in range(2):
                for g in range(NG):
                    raw_group(2 * i + p, g)
        act.wait_ge(angles_done, 1)
        act.activation(sin, sin, ACT.Sin).then_inc(rope_done, 1)
        act.activation(cos, cos, ACT.Sin).then_inc(rope_done, 1)
        for p in range(2):
            for g in range(NG):
                gate_group(GATE_BLOCK + p, g)
        b = RAW_BLOCKS - 2
        tile_in(0)
        gate_group(b, 0)
        gate_group(b, 1)
        high_parts(0)
        gate_group(b, 2)
        swapped_k(0)
        gate_group(b, 3)
        q_out(0)
        gate_group(b + 1, 0)
        k_out(0, 0)
        v_high(0, 0)
        for g in range(1, NG):
            gate_group(b + 1, g)

        with act.Fori(0, NT // 2) as i:
            for p in range(2):
                n = 2 * i + p

                def block_high(g):
                    act.wait_ge(proj_done, NG * (n + RAW_BLOCKS) + g + 1)
                    act.wait_ge(split_out[g % 2], 32 * (2 * n + g // 2))
                    act.activation(stage_hi[:, g % 2, :], bank[g][:, :], ACT.Copy).then_inc(hi_done, 1)

                tile_in(n + 1)
                softmax(n, 0)
                block_high(0)
                high_parts(n + 1)
                p_high(n, 0)
                swapped_k(n + 1)
                low_values(n, 0)
                block_high(1)
                y_high(n, 0)
                softmax(n, 1)
                q_out(n + 1)
                block_high(2)
                p_high(n, 1)
                k_out(n + 1, 1 - p)
                low_values(n, 1)
                y_high(n, 1)
                v_high(n + 1, 1 - p)
                block_high(3)

    @block.vector
    def _(dve):
        from concourse.bass import ds
        chain = Chain(dve, dve_chain)
        dve.wait_ge(consts_in, 64)
        norm_turn = 4
        with dve.Fori(0, NG) as g:
            chain.enter(g, norm_turn)
            dve.wait_ge(ssq_done, TPG * (g + 1))
            dve.tensor_scalar(ms[:, 0:TPG], ssq[:, 0:TPG], 1.0 / D_MODEL, EPS, ALU.mult, ALU.add).then_inc(ms_done, 1)
            dve.wait_ge(pow_done, g + 1)
            newton_rsqrt(dve, chain, rs[:, 0:TPG], ms[:, 0:TPG], rtmp[:, 0:TPG])
            for a in range(TPG):
                dve.tensor_scalar(x_in[:, a, :], x_in[:, a, :], rs[:, a:a + 1], None, ALU.mult).then_inc(x_scaled, 1)
            for k in range(KB):
                dve.wait_ge(ht_hi_done, KB * g + k + 1)
                at = ds(g * GRP, GRP)
                dve.scalar_tensor_tensor(ht_lo[:, k, at], xbank[k], gain[:, k:k + 1], ht_hi[:, k, at].bitcast(F32),
                                         ALU.mult, ALU.subtract).then_inc(ht_lo_done, 1)
        chain.leave(NG)

        ang, turns, tmp = rope_tmp
        flat = lambda v: v.rearrange("p a b -> p (a b)")
        dve.wait_ge(pos_in, 16)
        dve.wait_ge(consts_made, 2)
        chain.link(dve.tensor_copy(pos[:, :], pos_i[:, :]))
        dve.wait_ge(xt_done, KB * NG)
        dve.wait_ge(x_scaled, TPG * NG)
        chain.link(dve.tensor_tensor(ang, spread(pos[:, :], HALF, 2), spread(inv_freq[:, :], NT, 1), ALU.mult))
        for whole in (4096.0, 1.0):
            chain.link(dve.tensor_scalar(flat(turns), flat(ang), 1.0 / (2 * np.pi * whole), ROUND, ALU.mult, ALU.add))
            chain.link(dve.tensor_scalar(flat(turns), flat(turns), -ROUND, None, ALU.add))
            for part in TWO_PI_PARTS:
                chain.link(dve.scalar_tensor_tensor(flat(ang), flat(turns), -part * whole, flat(ang), ALU.mult, ALU.add))
        chain.link(dve.tensor_scalar(flat(sin), flat(ang), PI, -PI, ALU.min, ALU.max))
        chain.link(dve.tensor_scalar(flat(cos), flat(ang), np.pi / 2, None, ALU.add))
        chain.link(dve.tensor_scalar(flat(tmp), flat(cos), PI, -2 * np.pi, ALU.is_gt, ALU.mult))
        chain.link(dve.tensor_tensor(flat(cos), flat(cos), flat(tmp), ALU.add))
        dve.tensor_scalar(flat(cos), flat(cos), PI, -PI, ALU.min, ALU.max).then_inc(angles_done, 1)

        def gate_groups(m):
            for g in range(NG):
                dve.wait_ge(sigmoid_done, NG * m + g + 1)
                dve.tensor_tensor(stage_raw[:, g, :], bank[g][:, :], stage_raw[:, g, :], ALU.mult).then_inc(raw_done, 1)

        def v_low(n, p):
            dve.wait_ge(v_hi_done, n + 1)
            dve.tensor_tensor(v_s[:, p, :, HD:P], v_raw, v_s[:, p, :, 0:HD].bitcast(F32),
                              ALU.subtract).then_inc(v_done, 1)

        def norm_and_rotate(tile, n):
            dve.wait_ge(qk_out, n + 1)
            rot_all = rot.rearrange("p a (h d) -> p (a h) d", d=HD)
            chain.link(dve.tensor_tensor(rot_all, qk, qk, ALU.mult))
            chain.link(dve.tensor_reduce(ssq[:, :], rot_all, AX.X, ALU.add))
            dve.tensor_scalar(ms[:, :], ssq[:, :], 1.0 / HD, EPS, ALU.mult, ALU.add).then_inc(ms_done, 1)
            dve.wait_ge(pow_done, NG + n + 1)
            newton_rsqrt(dve, chain, rs[:, :], ms[:, :], rtmp[:, :])
            chain.link(dve.tensor_tensor(qk, qk, spread(rs[:, :], HD, 2), ALU.mult))
            dve.tensor_tensor(qk[:, 0:SWA_Q, :], qk[:, 0:SWA_Q, :], spread(qk_gain[:, 0, :], SWA_Q, 1), ALU.mult)
            chain.link(dve.tensor_tensor(qk[:, SWA_Q:, :], qk[:, SWA_Q:, :], spread(qk_gain[:, 1, :], SWA_KV, 1),
                                         ALU.mult))
            c_t = spread(cos[:, tile, :], QK, 1)
            s_t = spread(sin[:, tile, :], QK, 1)
            x1, x2 = qk[:, :, 0:HALF], qk[:, :, HALF:HD]
            dve.tensor_tensor(rot1, x1, c_t, ALU.mult)
            chain.link(dve.tensor_tensor(rot2, x2, s_t, ALU.mult))
            chain.link(dve.tensor_tensor(rot1, rot1, rot2, ALU.subtract))
            dve.tensor_tensor(x2, x2, c_t, ALU.mult)
            chain.link(dve.tensor_tensor(rot2, x1, s_t, ALU.mult))
            dve.tensor_tensor(x2, x2, rot2, ALU.add).then_inc(rot_done, 1)

        def low_parts(n):
            dve.wait_ge(qs_hi_done, 2 * (n + 1))
            dve.wait_ge(rot_done, n + 1)
            dve.tensor_tensor(qk_split[:, 0:QK, HD:HD + HALF], rot1, qk_split[:, 0:QK, 0:HALF].bitcast(F32), ALU.subtract)
            dve.tensor_tensor(qk_split[:, 0:QK, HD + HALF:P], qk[:, :, HALF:HD],
                              qk_split[:, 0:QK, HALF:HD].bitcast(F32), ALU.subtract).then_inc(qs_lo_done, 1)

        def top_score(n, half):
            dve.wait_ge(sc_done, 2 * n + half + 1)
            sinks = sink[:, GQ * half:GQ * half + GQ]
            chain.link(dve.tensor_reduce(top[:, :], Y[:, :].rearrange("p (a b) -> p a b", a=GQ), AX.X, ALU.max))
            chain.link(dve.scalar_tensor_tensor(top[:, :], top[:, :], SCALE, sinks, ALU.mult, ALU.max))
            dve.tensor_scalar(neg_top[:, :], top[:, :], -1.0, None, ALU.mult)
            dve.tensor_tensor(sink_e[:, :], sinks, top[:, :], ALU.subtract).then_inc(top_done, 1)

        def normalise(n, half):
            dve.wait_ge(exp_done, 2 * n + half + 1)
            chain.link(dve.tensor_tensor(den[:, :], den[:, :], sink_e[:, :], ALU.add))
            chain.link(dve.reciprocal(den[:, :], den[:, :]))
            dve.tensor_tensor(probs, probs, spread(den[:, :], 2 * P, 2), ALU.mult).then_inc(p_done, 1)

        def p_low(n, half):
            dve.wait_ge(p_hi_done, 2 * n + half + 1)
            dve.tensor_tensor(p_lo[:, :], Y[:, :], p_hi[:, :].bitcast(F32), ALU.subtract).then_inc(p_split, 1)

        def weighted(n, half):
            dve.wait_ge(yv_done, 2 * n + half + 1)
            dve.tensor_tensor(y_sum, y_sum, Y[0:HD, 0:GRP].rearrange("p (a b) -> p a b", a=GQ),
                              ALU.add).then_inc(y_read, 1)
            dve.wait_ge(y_read, 2 * n + half + 1)
            dve.tensor_tensor(y_sum, y_sum, gate_t[:, GQ * half:GQ * half + GQ, :], ALU.mult).then_inc(y_gated, 1)

        def y_low(n, half):
            dve.wait_ge(y_hi_done, 2 * n + half + 1)
            dve.tensor_tensor(y_lo, y_sum.rearrange("p a b -> p (a b)"), y_hi.bitcast(F32),
                              ALU.subtract).then_inc(y_done, 1)

        gate_groups(0)
        gate_groups(1)
        dve.wait_ge(rope_done, 2)
        norm_and_rotate(0, 0)
        low_parts(0)
        gate_groups(2)
        v_low(0, 0)
        gate_groups(3)
        with dve.Fori(0, NT // 2) as i:
            chain.enter(i, 2 * SWA_TURN)
            for p in range(2):
                n = 2 * i + p
                nxt = (n + 1) % NT

                def block_low(g):
                    dve.wait_ge(hi_done, NG * n + g + 1)
                    dve.tensor_tensor(stage_lo[:, g % 2, :], bank[g][:, :], stage_hi[:, g % 2, :].bitcast(F32),
                                      ALU.subtract).then_inc(split_done, 1)

                top_score(n, 0)
                normalise(n, 0)
                norm_and_rotate(nxt, n + 1)
                block_low(0)
                low_parts(n + 1)
                p_low(n, 0)
                weighted(n, 0)
                block_low(1)
                y_low(n, 0)
                top_score(n, 1)
                normalise(n, 1)
                block_low(2)
                p_low(n, 1)
                weighted(n, 1)
                y_low(n, 1)
                v_low(n + 1, 1 - p)
                block_low(3)
        chain.leave(NT // 2)


SWA_TURN = 19


PAIRS = SEQ // (2 * P)
ZC = 1024


def chunks_of(a):
    keys = P * (a + 1)
    return [(k0, min(ZC, keys - k0)) for k0 in range(0, keys, ZC)]


class Sticks:

    UNITS = 2 * PAIRS
    Z_TURN = 2 * sum(len(chunks_of(a)) for a in range(NT))
    K_TURN = 2 * sum(j + 1 for j in range(PAIRS))
    V_TURN = 2 * NT // 4
    T_TURN = K_TURN + V_TURN

    def __init__(self):
        self.unit = [(n // PAIRS, PAIRS - 1 - n % PAIRS) for n in range(self.UNITS)]
        self.z0, z = {}, 0
        self.k0, k = {}, 0
        for n, (_, j) in enumerate(self.unit):
            for s in range(2):
                self.z0[n, s] = z
                z += len(chunks_of(2 * j + s))
            self.k0[n] = k
            k += j + 1

    def unit_chunks(self, n):
        return self.unit[n][1] + 1

    def t_of(self, n, m):
        return self.k0[n] + m + self.V_TURN // 2 * (1 + self.unit[n][0])

    def v_chunk(self, head, m):
        return head * self.T_TURN // 2 + m

    def halves(self, n):
        j = self.unit[n][1]
        return range(0, (j + 1) // 2), range((j + 1) // 2, j + 1)


def sticks(nc, c, t):
    from concourse.bass import ds
    o = Sticks()
    sb = lambda n, s, d=F32: c.enter_context(nc.sbuf_tensor(n, s, d))
    sem = lambda n: c.enter_context(nc.semaphore(n))
    q_s = sb("q_s", [P, 2, SEQ], F32R)
    k_s = sb("k_s", [P, 2, 2, SEQ], F32R)
    v_t = sb("v_t", [P, 2, SEQ])
    v_s = sb("vb_s", [P, 2, NT, P], F32R)
    take = sb("take", [P, 4, SEQ])
    left = sb("left", [P, 2, SEQ])
    wt_hi, wt_lo = sb("wt_hi", [P, 2, 4 * P], F32R), sb("wt_lo", [P, 2, 4 * P], F32R)
    gate, gate_lo = sb("gate", [P, SEQ]), sb("gate_lo", [P, SEQ])
    y_sum = sb("yb_sum", [P, 2, 2 * P])
    y_hi, y_lo = sb("yb_hi", [P, 2, 2 * P], F32R), sb("yb_lo", [P, 2, 2 * P], F32R)
    ident, ident_bf = sb("identb", [P, P]), sb("identb_bf", [P, P], BF16)
    mask = sb("mask", [P, P], BF16)
    Z = [c.enter_context(nc.psum_tensor(f"Z{s}", [P, ZC], F32)) for s in range(2)]
    T = [c.enter_context(nc.psum_tensor(f"T{s}", [P, 4 * P], F32)) for s in range(2)]
    O = [c.enter_context(nc.psum_tensor(f"O{s}", [P, 4 * P], F32)) for s in range(2)]
    consts, chain_sem = sem("b_consts"), sem("b_chain")
    head_in = [sem(f"head_in{p}") for p in range(2)]
    gate_in, gate_sum, gate_sig, gate_done = sem("b_gate_in"), sem("gate_sum"), sem("gate_sig"), sem("gate_done")
    z_done, z_read, scanned, w_done = sem("z_done"), sem("z_read"), sem("scanned"), sem("w_done")
    t_done, wt_hi_done, t_read, pv_done = (sem(n) for n in ("t_done", "wt_hi_done", "t_read", "b_pv_done"))
    o_moved, o_read, y_gated, y_hi_done, y_done = (sem(n) for n in (
        "o_moved", "o_read", "b_y_gated", "b_y_hi_done", "b_y_done"))
    y_out = [sem(f"b_y_out{s}") for s in range(2)]
    y_seen = sem("b_y_seen")
    CREDIT = 2
    PV_CREDIT = o.unit_chunks(o.UNITS - 2) + o.unit_chunks(o.UNITS - 1)
    TURNS = SB_H // 2
    HB = SB_H * HD
    block = c.enter_context(nc.Block())

    @block.sync
    def _(sp):
        def rows(name, kind, head):
            return t[name][ds(kind * HB + head * HD, HD), :]

        def load_head(head, p):
            for half, (first, second) in enumerate((("hi", "lo"), ("lo", "hi"))):
                at = slice(half * HD, half * HD + HD)
                sp.dma_start(q_s[at, p, :].bitcast(F32), rows(first, 0, head)).then_inc(head_in[p], 16)
                sp.dma_start(k_s[at, p, 0, :].bitcast(F32), rows(first, 1, head)).then_inc(head_in[p], 16)
                sp.dma_start(k_s[at, p, 1, :].bitcast(F32), rows(second, 1, head)).then_inc(head_in[p], 16)
                sp.dma_start(v_t[at, p, :], rows(first, 2, head)).then_inc(head_in[p], 16)

        def load_gate(pair):
            sp.dma_start(gate[:, :], t["hi"][ds(3 * HB + pair * P, P), :]).then_inc(gate_in, 16)
            sp.dma_start(gate_lo[:, :], t["lo"][ds(3 * HB + pair * P, P), :]).then_inc(gate_in, 16)

        def store_y(i, n):
            p, j = o.unit[n]
            at = slice(p * HD, p * HD + HD)
            sp.wait_ge(y_done, o.UNITS * i + n + 1)
            sp.sem_inc(y_seen, 1)
            for y, d in ((y_hi, "y_hi"), (y_lo, "y_lo")):
                sp.dma_start(t[d][ds(SWA_Q * HD + i * P + p * HD, HD), j * 2 * P:(j + 1) * 2 * P],
                             y[at, n % 2, :].bitcast(F32)).then_inc(y_out[n % 2], 16)

        def turn(i, more):
            for p in range(2):
                for n in range(PAIRS * p, PAIRS * p + PAIRS):
                    store_y(i, n)
                if more:
                    sp.wait_ge(z_done, o.Z_TURN * i + o.Z_TURN // 2 * (p + 1))
                    load_head(2 * i + 2 + p, p)
            if more:
                load_gate(i + 1)

        load_head(0, 0)
        load_gate(0)
        load_head(1, 1)
        with sp.Fori(0, TURNS - 1) as i:
            turn(i, True)
        turn(TURNS - 1, False)
        for s in range(2):
            sp.wait_ge(y_out[s], 16 * 2 * TURNS * o.UNITS // 2)

    @block.gpsimd
    def _(pool):
        chain = Chain(pool, chain_sem)
        chain.link(pool.memset(ident[:, :], 0.0))
        chain.link(pool.affine_select(out=ident[:, :], in_=ident[:, :], compare_op=ALU.not_equal, fill=1.0,
                                      base=0, pattern=[[-1, P]], channel_multiplier=1))
        chain.link(pool.tensor_copy(ident_bf[:, :], ident[:, :]))
        chain.link(pool.memset(mask[:, :], 0.0))
        pool.affine_select(out=mask[:, :], in_=mask[:, :], compare_op=ALU.is_gt, fill=MASKED, base=0,
                           pattern=[[-1, P]], channel_multiplier=1).then_inc(consts, 1)

    @block.tensor
    def _(pe):
        mm = pe.matmul

        def scores(i, n, s):
            p, j = o.unit[n]
            a = 2 * j + s
            for m, (k0, keys) in enumerate(chunks_of(a)):
                z = o.z0[n, s] + m
                pe.wait_ge(z_read, CREDIT + o.Z_TURN * i + z - 1)
                for at in range(0, keys, GRP):
                    w = min(GRP, keys - at)
                    last = k0 + at + w == P * (a + 1)
                    for part in range(2):
                        ins = mm(Z[z % 2][:, at:at + w], q_s[:, p, a * P:(a + 1) * P],
                                 k_s[:, p, part, k0 + at:k0 + at + w], start=part == 0, stop=part == 1 and not last)
                    if last:
                        ins = mm(Z[z % 2][:, at + w - P:at + w], ident_bf[:, :], mask[:, :], start=False, stop=True)
                ins.then_inc(z_done, 1)

        def transpose_v(i, p):
            for m in range(NT // 4):
                x = o.v_chunk(p, m)
                pe.wait_ge(t_read, CREDIT + o.T_TURN * i + x - 1)
                for b in range(4):
                    ins = pe.transpose(T[x % 2][:, b * P:(b + 1) * P], v_t[:, p, (4 * m + b) * P:(4 * m + b + 1) * P],
                                       ident[:, :])
                ins.then_inc(t_done, 1)

        def transpose_w(i, n, m):
            j = o.unit[n][1]
            x = o.t_of(n, m)
            pe.wait_ge(t_read, CREDIT + o.T_TURN * i + x - 1)
            blocks = [(2 * m, 0), (2 * m, 1), (2 * m + 1, 0), (2 * m + 1, 1)]
            if m == j:
                blocks.remove((2 * m + 1, 0))
            for b, (kb, s) in enumerate(blocks):
                ins = pe.transpose(T[x % 2][:, b * P:(b + 1) * P], take[:, (2 * n + s) % 4, kb * P:(kb + 1) * P],
                                   ident[:, :])
            ins.then_inc(t_done, 1)

        def values(i, n, m):
            p, j = o.unit[n]
            x, k = o.t_of(n, m), o.k0[n] + m
            pe.wait_ge(t_read, CREDIT + o.T_TURN * i + x + 1)
            if m == 0:
                pe.wait_ge(o_read, CREDIT + o.UNITS * i + n - 1)
            for b in range(2):
                kb = 2 * m + b
                at, first = (2 * P, P) if m == j and b else (b * 2 * P, 0)
                for part, w in enumerate((wt_hi, wt_lo)):
                    ins = mm(O[n % 2][:, first:2 * P], v_s[:, p, kb, :], w[:, k % 2, at:at + 2 * P - first],
                             start=kb == 0 and part == 0, stop=m == j and b == 1 and part == 1)
            ins.then_inc(pv_done, 1)

        pe.wait_ge(consts, 1)
        with pe.Fori(0, TURNS) as i:
            for p in range(2):
                if p == 0:
                    pe.wait_ge(head_in[0], 128 * (i + 1))
                    transpose_v(i, 0)
                    for s in range(2):
                        scores(i, 0, s)
                for n in range(PAIRS * p, PAIRS * p + PAIRS):
                    if n == PAIRS:
                        transpose_v(i, 1)
                    for s, half in enumerate(o.halves(n)):
                        if n + 1 < o.UNITS:
                            if n + 1 == PAIRS and s == 0:
                                pe.wait_ge(head_in[1], 128 * (i + 1))
                            scores(i, n + 1, s)
                        if s == 0:
                            pe.wait_ge(w_done, CREDIT + 2 * o.UNITS * i + 2 * n + 2)
                        for m in half:
                            transpose_w(i, n, m)
                            if m:
                                values(i, n, m - 1)
                    values(i, n, o.unit[n][1])

    @block.scalar
    def _(act):
        for s in (z_read, t_read, w_done, o_read):
            act.sem_inc(s, CREDIT)
        act.sem_inc(pv_done, PV_CREDIT)

        def sigmoids(i, n, s):
            a = 2 * o.unit[n][1] + s
            tile = 2 * n + s
            if s == 0:
                before = o.k0[n - 1] if n else -o.unit_chunks(o.UNITS - 1)
                act.wait_ge(pv_done, PV_CREDIT + o.K_TURN * i + before)
            act.wait_ge(w_done, CREDIT + 2 * o.UNITS * i + tile - 1)
            for m, (k0, keys) in enumerate(chunks_of(a)):
                z = o.z0[n, s] + m
                act.wait_ge(z_done, o.Z_TURN * i + z + 1)
                act.activation(take[:, tile % 4, k0:k0 + keys], Z[z % 2][:, 0:keys], ACT.Sigmoid, scale=SCALE)
                act.activation(left[:, tile % 2, k0:k0 + keys], Z[z % 2][:, 0:keys], ACT.Sigmoid,
                               scale=-SCALE).then_inc(z_read, 1)

        def high(i, n, m):
            x, k = o.t_of(n, m), o.k0[n] + m
            w = 3 * P if m == o.unit[n][1] else 4 * P
            act.wait_ge(t_done, o.T_TURN * i + x + 1)
            act.wait_ge(pv_done, PV_CREDIT + o.K_TURN * i + k - 1)
            act.activation(wt_hi[:, k % 2, 0:w], T[x % 2][:, 0:w], ACT.Copy).then_inc(wt_hi_done, 1)

        def move_part(i, n):
            p = o.unit[n][0]
            act.wait_ge(pv_done, PV_CREDIT + o.K_TURN * i + o.k0[n] + o.unit_chunks(n))
            act.wait_ge(y_out[n % 2], 32 * (o.UNITS // 2 * i + n // 2))
            act.activation(y_sum[p * HD:p * HD + HD, n % 2, :], O[n % 2][HD - p * HD:P - p * HD, 0:2 * P],
                           ACT.Copy).then_inc(o_moved, 1)

        def y_high(i, n):
            p = o.unit[n][0]
            at = slice(p * HD, p * HD + HD)
            act.wait_ge(y_gated, o.UNITS * i + n + 1)
            act.activation(y_hi[at, n % 2, :], y_sum[at, n % 2, :], ACT.Copy).then_inc(y_hi_done, 1)

        with act.Fori(0, TURNS) as i:
            for s in range(2):
                sigmoids(i, 0, s)
            act.wait_ge(gate_sum, i + 1)
            act.wait_ge(gate_done, i)
            act.activation(gate_lo[:, :], gate[:, :], ACT.Sigmoid).then_inc(gate_sig, 1)
            for n in range(o.UNITS):
                for s, half in enumerate(o.halves(n)):
                    if n + 1 < o.UNITS:
                        sigmoids(i, n + 1, s)
                    if n and s == 0:
                        move_part(i, n - 1)
                    if n and s == 1:
                        y_high(i, n - 1)
                    for m in half:
                        high(i, n, m)
            move_part(i, o.UNITS - 1)
            y_high(i, o.UNITS - 1)

    @block.vector
    def _(dve):
        def weights(i, n, s):
            a = 2 * o.unit[n][1] + s
            keys, tile = P * (a + 1), 2 * n + s
            dve.wait_ge(z_read, CREDIT + o.Z_TURN * i + o.z0[n, s] + len(chunks_of(a)))
            back = left[:, tile % 2, 0:keys][:, ::-1]
            dve.tensor_tensor_scan(back, back, back, 1.0, ALU.mult, ALU.min).then_inc(scanned, 1)
            dve.wait_ge(scanned, 2 * o.UNITS * i + tile + 1)
            dve.tensor_tensor(take[:, tile % 4, 0:keys - 1], take[:, tile % 4, 0:keys - 1],
                              left[:, tile % 2, 1:keys], ALU.mult).then_inc(w_done, 1)

        def copy_v(i, p):
            for m in range(NT // 4):
                x = o.v_chunk(p, m)
                dve.wait_ge(t_done, o.T_TURN * i + x + 1)
                dve.tensor_copy(v_s[:, p, 4 * m:4 * m + 4, :].rearrange("p a b -> p (a b)"),
                                T[x % 2][:, :]).then_inc(t_read, 1)

        def low(i, n, m):
            x, k = o.t_of(n, m), o.k0[n] + m
            w = 3 * P if m == o.unit[n][1] else 4 * P
            dve.wait_ge(wt_hi_done, o.K_TURN * i + k + 1)
            dve.tensor_tensor(wt_lo[:, k % 2, 0:w], T[x % 2][:, 0:w], wt_hi[:, k % 2, 0:w].bitcast(F32),
                              ALU.subtract).then_inc(t_read, 1)

        def gated_sum(i, n):
            p, j = o.unit[n]
            at = slice(p * HD, p * HD + HD)
            y = y_sum[at, n % 2, :]
            dve.wait_ge(o_moved, o.UNITS * i + n + 1)
            dve.tensor_tensor(y, O[n % 2][at, 0:2 * P], y, ALU.add).then_inc(o_read, 1)
            dve.wait_ge(o_read, CREDIT + o.UNITS * i + n + 1)
            dve.tensor_tensor(y, y, gate[at, j * 2 * P:(j + 1) * 2 * P], ALU.mult).then_inc(y_gated, 1)

        def y_low(i, n):
            p = o.unit[n][0]
            at = slice(p * HD, p * HD + HD)
            dve.wait_ge(y_hi_done, o.UNITS * i + n + 1)
            dve.tensor_tensor(y_lo[at, n % 2, :], y_sum[at, n % 2, :], y_hi[at, n % 2, :].bitcast(F32),
                              ALU.subtract).then_inc(y_done, 1)

        with dve.Fori(0, TURNS) as i:
            dve.wait_ge(gate_in, 32 * (i + 1))
            dve.tensor_tensor(gate[:, :], gate[:, :], gate_lo[:, :], ALU.add).then_inc(gate_sum, 1)
            copy_v(i, 0)
            for s in range(2):
                weights(i, 0, s)
            dve.wait_ge(gate_sig, i + 1)
            dve.tensor_tensor(gate[:, :], gate[:, :], gate_lo[:, :], ALU.mult).then_inc(gate_done, 1)
            dve.wait_ge(gate_done, i + 1)
            for n in range(o.UNITS):
                if n == PAIRS:
                    copy_v(i, 1)
                for s, half in enumerate(o.halves(n)):
                    if n and s == 0:
                        gated_sum(i, n - 1)
                    for m in half:
                        low(i, n, m)
                    if n and s == 1:
                        y_low(i, n - 1)
                    if n + 1 < o.UNITS:
                        weights(i, n + 1, s)
            gated_sum(i, o.UNITS - 1)
            y_low(i, o.UNITS - 1)


def mix_out(nc, c, t):
    from concourse.bass import ds
    sb = lambda n, s, d=F32: c.enter_context(nc.sbuf_tensor(n, s, d))
    sem = lambda n: c.enter_context(nc.semaphore(n))
    w_raw = sb("wo_raw", [P, 2, D_MODEL])
    w_hi, w_lo = sb("wo_hi", [P, KB, D_MODEL], F32R), sb("wo_lo", [P, KB, D_MODEL], F32R)
    y_t = [sb(n, [P, 2, KB, P], F32R) for n in ("yt_hi", "yt_lo")]
    x_t, out_t = sb("x_t", [P, 2, D_MODEL]), sb("out_t", [P, 2, D_MODEL])
    bank = [c.enter_context(nc.psum_tensor(f"obank{n}", [P, GRP], F32)) for n in range(4)]
    w_in = [sem(f"wo_in{s}") for s in range(2)]
    w_hi_done, w_lo_done = sem("wo_hi_done"), sem("wo_lo_done")
    y_in = [sem(f"y_in{s}") for s in range(2)]
    x_in = [sem(f"xo_in{s}") for s in range(2)]
    tile_done, out_done = sem("tile_done"), sem("out_done")
    out_out = [sem(f"out_out{s}") for s in range(2)]
    HALVES = D_MODEL // GRP
    block = c.enter_context(nc.Block())
    w_view = t["w_out"].rearrange("l (k p) n -> p (l k) n", p=P)
    y_views = [t[n].rearrange("(k p) t -> p k t", p=P) for n in ("y_hi", "y_lo")]

    @block.sync
    def _(sp):
        def load(tile, s):
            for y, v in zip(y_t, y_views):
                sp.dma_start(y[:, s].bitcast(F32), v[:, :, ds(tile * P, P)]).then_inc(y_in[s], 16)
            sp.dma_start(x_t[:, s, :], t["x"][0, ds(tile * P, P), :]).then_inc(x_in[s], 16)

        for k in range(KB):
            if k >= 2:
                sp.wait_ge(w_lo_done, k - 1)
            sp.dma_start(w_raw[:, k % 2, :], w_view[:, k, :]).then_inc(w_in[k % 2], 16)
            if k == 1:
                load(0, 0)
                load(1, 1)

        def turn(i, more):
            for s in range(2):
                n = 2 * i + s
                sp.wait_ge(out_done, HALVES * (n + 3))
                sp.dma_start(t["out"][0, ds(n * P, P), :], out_t[:, s, :]).then_inc(out_out[s], 16)
                if more:
                    load(n + 2, s)

        with sp.Fori(0, NT // 2 - 1) as i:
            turn(i, True)
        turn(NT // 2 - 1, False)
        for s in range(2):
            sp.wait_ge(out_out[s], 16 * NT // 2)

    @block.scalar
    def _(act):
        for k in range(KB):
            act.wait_ge(w_in[k % 2], 16 * (k // 2 + 1))
            act.activation(w_hi[:, k, :], w_raw[:, k % 2, :], ACT.Copy).then_inc(w_hi_done, 1)

    @block.tensor
    def _(pe):
        pe.sem_inc(out_done, 2 * HALVES)
        pe.wait_ge(w_lo_done, KB)
        with pe.Fori(0, NT // 2) as i:
            for s in range(2):
                n = 2 * i + s
                pe.wait_ge(y_in[s], 32 * (i + 1))
                passes = [(y, w, k) for y, w in ((0, w_hi), (0, w_lo), (1, w_hi)) for k in range(KB)]
                for h in range(HALVES):
                    pe.wait_ge(out_done, HALVES * n + h + 1)
                    for m, (y, w, k) in enumerate(passes):
                        ins = pe.matmul(bank[2 * s + h][:, :], y_t[y][:, s, k, :], w[:, k, h * GRP:(h + 1) * GRP],
                                        start=m == 0, stop=m == len(passes) - 1)
                    ins.then_inc(tile_done, 1)

    @block.vector
    def _(dve):
        for k in range(KB):
            dve.wait_ge(w_hi_done, k + 1)
            dve.tensor_tensor(w_lo[:, k, :], w_raw[:, k % 2, :], w_hi[:, k, :].bitcast(F32),
                              ALU.subtract).then_inc(w_lo_done, 1)
        with dve.Fori(0, NT // 2) as i:
            for s in range(2):
                n = 2 * i + s
                dve.wait_ge(x_in[s], 16 * (i + 1))
                dve.wait_ge(out_out[s], 16 * i)
                for h in range(HALVES):
                    at = slice(h * GRP, (h + 1) * GRP)
                    dve.wait_ge(tile_done, HALVES * n + h + 1)
                    dve.tensor_tensor(out_t[:, s, at], bank[2 * s + h][:, :], x_t[:, s, at],
                                      ALU.add).then_inc(out_done, 1)


def build(nc, t):
    for stage in (project, sticks, mix_out):
        with ExitStack() as c:
            stage(nc, c, t)


def kernel(**inputs):
    import concourse.bacc as bacc
    from concourse.bass_utils import run_bass_kernel_spmd

    nc = bacc.Bacc("TRN2", target_bir_lowering=False, num_devices=1)
    arrays, t = {}, {}
    for name in ("x", "positions", "norm_gain", "w_in", "q_norm_gain", "k_norm_gain", "sinks", "w_out"):
        a = np.ascontiguousarray(inputs[name])
        arrays[f"in_{name}"] = a
        t[name] = nc.dram_tensor(f"in_{name}", a.shape, mybir.dt.from_np(a.dtype), kind="ExternalInput").ap()
    for name, rows in (("raw", RAW_BLOCKS * P), ("hi", SPLIT_BLOCKS * P), ("lo", SPLIT_BLOCKS * P),
                       ("y_hi", D_MODEL), ("y_lo", D_MODEL)):
        t[name] = nc.dram_tensor(f"scratch_{name}", (rows, SEQ), F32).ap()
    t["out"] = nc.dram_tensor("out", (1, SEQ, D_MODEL), F32, kind="ExternalOutput").ap()
    build(nc, t)
    r = run_bass_kernel_spmd(nc, [arrays], core_ids=[0])
    return r.results[0]["out"]
```

```python
from contextlib import ExitStack

import numpy as np
from concourse import mybir

F32 = mybir.dt.float32
F32R = mybir.dt.float32r
BF16 = mybir.dt.bfloat16
I32 = mybir.dt.int32
ALU = mybir.AluOpType
ACT = mybir.ActivationFunctionType
AX = mybir.AxisListType

P = 128
SEQ, D_MODEL = 2048, 1024
HD = 64
HALF = HD // 2
KB = D_MODEL // P
GRP = 512
NG = SEQ // GRP
NT = SEQ // P
TPG = GRP // P
SWA_Q, SWA_KV, SB_H = 8, 2, 8
GQ = SWA_Q // SWA_KV
RAW_BLOCKS = 10
GATE_BLOCK = 6
SPLIT_BLOCKS = 16
QK = SWA_Q + SWA_KV
EPS = 1e-6
SCALE = HD ** -0.5
MASKED = -1e30
THETA = 10000.0
PI = float(np.float32(3.1415925))
TWO_PI_PARTS = (6.25, 0.033203125, -1.7881393432617188e-05, 2 * np.pi - 6.25 - 0.033203125 + 1.7881393432617188e-05)
ROUND = float(1.5 * 2 ** 23)


def view(buf, at, shape):
    n = int(np.prod(shape))
    v = buf[:, at:at + n]
    if len(shape) == 2:
        v = v.rearrange("p (a b) -> p a b", a=shape[0])
    return v


def spread(ap, n, where):
    shape = list(ap.shape)
    shape.insert(where, n)
    return ap.unsqueeze(where).broadcast_to(shape)


class Chain:

    def __init__(self, eng, sem):
        self.eng, self.sem, self.n, self.turn = eng, sem, 0, 0

    def link(self, ins):
        ins.then_inc(self.sem, 1)
        self.n += 1
        self.eng.wait_ge(self.sem, self.turn + self.n)

    def enter(self, i, per_turn):
        self.turn, self.base, self.per_turn = i * per_turn, self.n, per_turn

    def leave(self, turns):
        assert self.n - self.base == self.per_turn, (self.n - self.base, self.per_turn)
        self.turn, self.n = 0, self.base + turns * self.per_turn


def newton_rsqrt(dve, chain, y, ms, tmp):
    chain.link(dve.tensor_tensor(tmp, y, y, ALU.mult))
    chain.link(dve.tensor_tensor(tmp, tmp, ms, ALU.mult))
    chain.link(dve.tensor_scalar(tmp, tmp, -0.5, 1.5, ALU.mult, ALU.add))
    chain.link(dve.tensor_tensor(y, y, tmp, ALU.mult))


def project(nc, c, t):
    sb = lambda n, s, d=F32: c.enter_context(nc.sbuf_tensor(n, s, d))
    sem = lambda n: c.enter_context(nc.semaphore(n))
    ht_hi, ht_lo = sb("ht_hi", [P, KB, SEQ], F32R), sb("ht_lo", [P, KB, SEQ], F32R)
    w_hi, w_lo = sb("w_hi", [P, 2, KB, P], F32R), sb("w_lo", [P, 2, KB, P], F32R)
    w_raw = sb("w_raw", [P, 2, KB // 2, P])
    arena = sb("arena", [P, 5248])
    x_in = view(arena, 0, (TPG, D_MODEL))
    qkv_t = view(arena, 0, (6, P))
    qkv = view(arena, 768, (QK + SWA_KV, HD))
    qk, v_raw = qkv[:, 0:QK, :], qkv[:, QK:, :]
    rot = view(arena, 1536, (2, QK * HALF))
    rot1, rot2 = (rot[:, n, :].rearrange("p (h d) -> p h d", h=QK) for n in range(2))
    probs = view(arena, 2176, (GQ, 2 * P))
    y_sum = view(arena, 2176, (GQ, P))[0:HD]
    gate_t = view(arena, 3200, (SWA_Q, P))[0:HD]
    stage_raw = view(arena, 2176, (NG, GRP))
    rope_tmp = [view(arena, 512 * n, (NT, HALF)) for n in range(3)]
    cos, sin = view(arena, 4224, (NT, HALF)), view(arena, 4736, (NT, HALF))
    stage_hi, stage_lo = sb("stage_hi", [P, 2, GRP], F32R), sb("stage_lo", [P, 2, GRP], F32R)
    qk_split = sb("qk_split", [P, QK + SWA_KV, P], F32R)
    q_t = sb("q_t", [P, SWA_Q, P], F32R)
    k_t = sb("k_t", [P, 2, SWA_KV, 2, P], F32R)
    v_s = sb("v_s", [P, 2, SWA_KV, P], F32R)
    p_hi, p_lo = sb("p_hi", [P, 2 * GQ * P], F32R), sb("p_lo", [P, 2 * GQ * P], F32R)
    ident, ident_bf = sb("ident", [P, P]), sb("ident_bf", [P, P], BF16)
    mask_even = sb("mask_even", [P, 2, 2 * P], BF16)
    mask_odd = sb("mask_odd", [P, 2 * P], BF16)
    gain = sb("gain", [P, KB])
    qk_gain = sb("qk_gain", [P, 2, HD])
    sink = sb("sink", [P, SWA_Q])
    inv_freq = sb("inv_freq", [P, HALF])
    pos_i, pos = sb("pos_i", [P, NT], I32), sb("pos", [P, NT])
    power = sb("power", [P, QK])
    ssq, ms, rs, rtmp = (sb(n, [P, QK]) for n in ("ssq", "ms", "rs", "rtmp"))
    top, neg_top, sink_e, den = (sb(n, [P, GQ]) for n in ("top", "neg_top", "sink_e", "den"))
    bank = [c.enter_context(nc.psum_tensor(f"bank{n}", [P, GRP], F32)) for n in range(4)]
    X = c.enter_context(nc.psum_tensor("X", [P, 2 * GRP], F32))
    Y = c.enter_context(nc.psum_tensor("Y", [P, 2 * GRP], F32))
    xbank = [b[:, :] for b in bank] + [X[:, 0:GRP], X[:, GRP:], Y[:, 0:GRP], Y[:, GRP:]]

    x_loaded = [sem(f"x_loaded{a}") for a in range(TPG)]
    consts_in, pos_in = sem("consts_in"), sem("pos_in")
    ssq_done, ms_done, pow_done, x_scaled = sem("ssq_done"), sem("ms_done"), sem("pow_done"), sem("x_scaled")
    x_used = sem("x_used")
    xt_done, ht_hi_done, ht_lo_done = sem("xt_done"), sem("ht_hi_done"), sem("ht_lo_done")
    pool_chain, dve_chain, act_chain = sem("pool_chain"), sem("dve_chain"), sem("act_chain")
    consts_made = sem("consts_made")
    w_loaded = [sem(f"w_loaded{h}") for h in range(2)]
    w_hi_done, w_split = sem("w_hi_done"), sem("w_split")
    sigmoid_done = sem("sigmoid_done")
    proj_done, raw_done, hi_done, split_done = sem("proj_done"), sem("raw_done"), sem("hi_done"), sem("split_done")
    raw_out = [sem(f"raw_out{g}") for g in range(NG)]
    split_out = [sem(f"split_out{s}") for s in range(2)]
    angles_done, rope_done = sem("angles_done"), sem("rope_done")
    qkv_in, gate_in = sem("qkv_in"), sem("gate_in")
    tin_done, qk_out, v_hi_done, v_done = sem("tin_done"), sem("qk_out"), sem("v_hi_done"), sem("v_done")
    rot_done, qs_hi_done, qs_lo_done, qs_done = sem("rot_done"), sem("qs_hi_done"), sem("qs_lo_done"), sem("qs_done")
    tq_done, q_ready, tk_done, k_ready = sem("tq_done"), sem("q_ready"), sem("tk_done"), sem("k_ready")
    sc_done, top_done, exp_done, p_done = sem("sc_done"), sem("top_done"), sem("exp_done"), sem("p_done")
    pt_done, p_hi_done, p_split = sem("pt_done"), sem("p_hi_done"), sem("p_split")
    pv_done, yv_done, y_read, y_gated = sem("pv_done"), sem("yv_done"), sem("y_read"), sem("y_gated")
    y_out = sem("y_out")
    w_seen, y_seen = sem("w_seen"), sem("y_seen")
    block = c.enter_context(nc.Block())

    w_view = t["w_in"].rearrange("l (k p) n -> p (l k) n", p=P)
    raw_view = t["raw"].rearrange("(b p) t -> p b t", p=P)
    gate_view = t["raw"][6 * P:RAW_BLOCKS * P, :].rearrange("(h d) t -> d h t", d=HD)
    y_view = t["y"][0:SWA_Q * HD, :].rearrange("(h d) t -> d h t", d=HD)

    @block.sync
    def _(sp):
        from concourse.bass import ds

        def load_x(a, tile):
            sp.dma_start(x_in[:, a, :], t["x"][0, ds(tile * P, P), :]).then_inc(x_loaded[a], 16)

        def load_w(b):
            for h in range(2):
                sp.dma_start(w_raw[:, h], w_view[:, 4 * h:4 * h + 4, ds(b * P, P)]).then_inc(w_loaded[h], 16)

        def prefetch_w(b):
            for h in range(2):
                sp.wait_ge(w_split, 2 * b + h + 1)
                sp.dma_start(w_raw[:, h], w_view[:, 4 * h:4 * h + 4, ds((b + 1) * P, P)]).then_inc(w_loaded[h], 16)

        for a in range(TPG):
            load_x(a, a)
        with nc.allow_non_contiguous_dma(reason="small columns of constants"):
            sp.dma_start(gain[:, :], t["norm_gain"].rearrange("l (k p) -> p (l k)", p=P)).then_inc(consts_in, 16)
            sp.dma_start(pos_i[:, :], t["positions"].rearrange("b (n p) -> p (b n)", p=P)).then_inc(pos_in, 16)
        sp.dma_start(qk_gain[:, 0, :], t["q_norm_gain"].broadcast_to([P, HD])).then_inc(consts_in, 16)
        sp.dma_start(qk_gain[:, 1, :], t["k_norm_gain"].broadcast_to([P, HD])).then_inc(consts_in, 16)
        sp.dma_start(sink[:, :], t["sinks"].broadcast_to([P, SWA_Q])).then_inc(consts_in, 16)
        load_w(0)
        with sp.Fori(1, NG) as g:
            for a in range(TPG):
                sp.wait_ge(*((x_used, g) if a < 2 else (xt_done, KB * g)))
                load_x(a, TPG * g + a)

        def raw_block(b):
            prefetch_w(b)
            for g in range(NG):
                sp.wait_ge(raw_done, NG + NG * b + g + 1)
                sp.dma_start(t["raw"][ds(b * P, P), g * GRP:(g + 1) * GRP],
                             stage_raw[:, g, :]).then_inc(raw_out[g], 16)

        with sp.Fori(0, RAW_BLOCKS // 2 - 1) as i:
            for p in range(2):
                raw_block(2 * i + p)

        def load_qkv(tile, n):
            sp.wait_ge(tin_done, n)
            sp.dma_start(qkv_t, raw_view[:, 0:6, ds(tile * P, P)]).then_inc(qkv_in, 16)

        def store_y(tile, half):
            n = 2 * tile + half
            sp.wait_ge(y_gated, 1 + n + 1)
            sp.sem_inc(y_seen, 1)
            sp.dma_start(y_view[:, GQ * half:GQ * half + GQ, ds(tile * P, P)],
                         gate_t[:, GQ * half:GQ * half + GQ, :]).then_inc(y_out, 16)

        def split_block(tile, more):
            if more:
                nxt = sp.snap((tile + 2) % NT)
                load_qkv(nxt, tile + 2)
                prefetch_w(tile + RAW_BLOCKS)
            sp.wait_ge(y_out, 16 + 16 * 2 * tile)
            sp.dma_start(gate_t, gate_view[:, :, ds(tile * P, P)]).then_inc(gate_in, 16)
            for g in range(NG):
                sp.wait_ge(split_done, NG + NG * tile + g + 1)
                for st, d in ((stage_hi, "hi"), (stage_lo, "lo")):
                    sp.dma_start(t[d][ds(tile * P, P), g * GRP:(g + 1) * GRP],
                                 st[:, g % 2, :].bitcast(F32)).then_inc(split_out[g % 2], 16)
                if g == 2:
                    store_y(tile, 0)
            store_y(tile, 1)

        for g in range(NG):
            sp.wait_ge(raw_out[g], 16 * (RAW_BLOCKS - 1))
        sp.wait_ge(angles_done, 1)
        load_qkv(0, 0)
        raw_block(RAW_BLOCKS - 2)
        load_qkv(1, 1)
        raw_block(RAW_BLOCKS - 1)
        for g in range(NG):
            sp.wait_ge(raw_out[g], 16 * (RAW_BLOCKS + 1))
        with sp.Fori(0, NT // 2 - 1) as i:
            for p in range(2):
                split_block(2 * i + p, True)
        split_block(NT - 2, True)
        split_block(NT - 1, False)
        sp.wait_ge(y_out, 16 + 16 * 2 * NT)
        for s in range(2):
            sp.wait_ge(split_out[s], 16 + 16 * 2 * 2 * NT)

    @block.gpsimd
    def _(pool):
        chain = Chain(pool, pool_chain)

        pool.memset(power[:, :], -0.5).then_inc(consts_made, 1)
        for n in range(HALF):
            ins = pool.memset(inv_freq[:, n:n + 1], float(np.float32(THETA) ** np.float32(-n * 2.0 / HD)))
        ins.then_inc(consts_made, 1)
        chain.link(pool.memset(ident[:, :], 0.0))
        chain.link(pool.affine_select(out=ident[:, :], in_=ident[:, :], compare_op=ALU.not_equal, fill=1.0,
                                      base=0, pattern=[[-1, P]], channel_multiplier=1))
        pool.tensor_copy(ident_bf[:, :], ident[:, :]).then_inc(consts_made, 1)

        with pool.Fori(0, NG) as g:
            pool.wait_ge(ms_done, g + 1)
            pool.tensor_tensor(rs[:, 0:TPG], ms[:, 0:TPG], power[:, 0:TPG], ALU.pow).then_inc(pow_done, 1)

        chain.link(pool.memset(mask_even[:, :, :], 0.0))
        chain.link(pool.memset(mask_odd[:, :], 0.0))
        own = dict(compare_op=ALU.is_ge, fill=MASKED, base=0, pattern=[[-1, P]], channel_multiplier=1)
        before = dict(compare_op=ALU.is_gt, fill=MASKED, base=0, pattern=[[1, P]], channel_multiplier=-1)
        for n in range(2):
            chain.link(pool.affine_select(out=mask_even[:, n, 0:P], in_=mask_even[:, n, 0:P], **own))
        chain.link(pool.memset(mask_even[:, 0, P:], MASKED))
        chain.link(pool.affine_select(out=mask_even[:, 1, P:], in_=mask_even[:, 1, P:], **before))
        chain.link(pool.affine_select(out=mask_odd[:, 0:P], in_=mask_odd[:, 0:P], **before))
        pool.affine_select(out=mask_odd[:, P:], in_=mask_odd[:, P:], **own).then_inc(consts_made, 1)
        pool.memset(k_t[:, :, :, 1, :].bitcast(F32), 0.0).then_inc(consts_made, 1)
        pool.memset(v_s[:, 1].bitcast(F32), 0.0).then_inc(consts_made, 1)

        def split_w(b, p, free):
            if free is not None:
                pool.wait_ge(proj_done, free)
            for h in range(2):
                at = slice(4 * h, 4 * h + 4)
                pool.wait_ge(w_loaded[h], 16 * (b + 1))
                pool.sem_inc(w_seen, 1)
                pool.tensor_copy(w_hi[:, p, at], w_raw[:, h]).then_inc(w_hi_done, 1)
                pool.wait_ge(w_hi_done, 2 * b + h + 1)
                pool.tensor_tensor(w_lo[:, p, at], w_raw[:, h], w_hi[:, p, at].bitcast(F32),
                                   ALU.subtract).then_inc(w_split, 1)

        split_w(0, 0, None)
        split_w(1, 1, None)

        with pool.Fori(1, RAW_BLOCKS // 2) as i:
            for p in range(2):
                split_w(2 * i + p, p, NG * (2 * i + p - 1))

        def qk_power(n):
            pool.wait_ge(ms_done, NG + n + 1)
            pool.tensor_tensor(rs[:, :], ms[:, :], power[:, :], ALU.pow).then_inc(pow_done, 1)

        qk_power(0)
        with pool.Fori(RAW_BLOCKS // 2, (RAW_BLOCKS + SPLIT_BLOCKS) // 2) as i:
            for p in range(2):
                split_w(2 * i + p, p, NG * (2 * i + p - 1))
                qk_power(2 * i + p - RAW_BLOCKS + 1)

    @block.tensor
    def _(pe):
        from concourse.bass import ds
        mm = pe.matmul
        pe.wait_ge(consts_made, 3)
        with pe.Fori(0, NG) as g:
            pe.wait_ge(ht_lo_done, 1 + KB * g)
            for pair in range(2):
                pe.wait_ge(x_scaled, TPG * g + 2 * pair + 2)
                for k in range(KB):
                    for a in (2 * pair, 2 * pair + 1):
                        ins = pe.transpose(xbank[k][:, a * P:(a + 1) * P], x_in[:, a, k * P:(k + 1) * P], ident[:, :])
                    if pair:
                        ins.then_inc(xt_done, 1)
                if not pair:
                    ins.then_inc(x_used, 1)
        pe.wait_ge(ht_lo_done, 1 + KB * NG)
        pe.wait_ge(consts_made, 6)

        def project_half(b, p, g, half):
            passes = [(w, h, k) for w, h in ((w_hi, ht_hi), (w_hi, ht_lo), (w_lo, ht_hi)) for k in range(KB)]
            for n in range(12 * half, 12 * half + 12):
                w, h, k = passes[n]
                ins = mm(bank[g][:, :], w[:, p, k, :], h[:, k, g * GRP:(g + 1) * GRP], start=n == 0, stop=n == 23)
            if half:
                ins.then_inc(proj_done, 1)

        def tokens_out(n):
            pe.wait_ge(qkv_in, 16 * (n + 1))
            pe.wait_ge(k_ready, n)
            for j in range(6):
                ins = pe.transpose(X[:, j * P:(j + 1) * P], qkv_t[:, j, :], ident[:, :])
            ins.then_inc(tin_done, 1)

        def q_columns(n):
            pe.wait_ge(qk_out, n + 1)
            pe.wait_ge(qs_done, n + 1)
            for j in range(SWA_Q):
                ins = pe.transpose(X[:, j * P:(j + 1) * P], qk_split[:, j, :].bitcast(F32), ident[:, :])
            ins.then_inc(tq_done, 1)

        def k_columns(n):
            pe.wait_ge(q_ready, n + 1)
            for j in range(2 * SWA_KV):
                ins = pe.transpose(X[:, j * P:(j + 1) * P], qk_split[:, SWA_Q + j, :].bitcast(F32), ident[:, :])
            ins.then_inc(tk_done, 1)

        def scores(n, half, mask):
            pe.wait_ge(k_ready, n + 1)
            pe.wait_ge(y_read, 1 + 2 * n + half)
            for j in range(GQ):
                out = Y[:, j * 2 * P:(j + 1) * 2 * P]
                mm(out, ident_bf[:, :], mask, start=True, stop=False)
                for s in range(2):
                    ins = mm(out, q_t[:, GQ * half + j, :], k_t[:, s, half, :, :].rearrange("p a b -> p (a b)"),
                             start=False, stop=s == 1)
            ins.then_inc(sc_done, 1)

        def probs_t(n, half):
            pe.wait_ge(p_done, 2 * n + half + 1)
            for s in range(2):
                for j in range(GQ):
                    at = (s * GQ + j) * P
                    ins = pe.transpose(Y[:, at:at + P], probs[:, j, s * P:(s + 1) * P], ident[:, :])
            ins.then_inc(pt_done, 1)

        def values(n, half):
            pe.wait_ge(v_done, n + 1)
            pe.wait_ge(p_split, 2 * n + half + 1)
            for s in range(2):
                for m, part in enumerate((p_hi, p_lo)):
                    ins = mm(Y[:, 0:GRP], v_s[:, s, half, :], part[:, s * GRP:(s + 1) * GRP],
                             start=s == 0 and m == 0, stop=s == 1 and m == 1)
            ins.then_inc(pv_done, 1)

        with pe.Fori(0, RAW_BLOCKS // 2 - 1) as i:
            for p in range(2):
                b = 2 * i + p
                pe.wait_ge(w_split, 2 * (b + 1))
                for g in range(NG):
                    pe.wait_ge(raw_done, NG * b + g + 1)
                    for half in range(2):
                        project_half(b, p, g, half)
        for p in range(2):
            b = RAW_BLOCKS - 2 + p
            pe.wait_ge(w_split, 2 * (b + 1))
            for g in range(NG):
                pe.wait_ge(raw_done, NG * b + g + 1)
                if (p, g) == (0, 0):
                    tokens_out(0)
                if (p, g) == (1, 0):
                    q_columns(0)
                if (p, g) == (1, 1):
                    k_columns(0)
                for half in range(2):
                    project_half(b, p, g, half)
        pe.wait_ge(raw_done, NG * (RAW_BLOCKS + 1))
        with pe.Fori(0, NT // 2) as i:
            for p in range(2):
                n = 2 * i + p
                b = n + RAW_BLOCKS
                if p:
                    mask = mask_odd[:, :]
                else:
                    mask = mask_even[:, :, :].rearrange("p a b -> p (a b)")[:, ds(((i + 7) // 8) * (2 * P), 2 * P)]
                pe.wait_ge(w_split, 2 * (b + 1))
                for h in range(2 * NG + 1):
                    if h == 0:
                        tokens_out(n + 1)
                    if h in (1, 5):
                        scores(n, h // 4, mask)
                    if h in (3, 7):
                        probs_t(n, h // 4)
                    if h in (4, 8):
                        values(n, h // 4 - 1)
                    if h == 6:
                        q_columns(n + 1)
                    if h == 7:
                        k_columns(n + 1)
                    if h < 2 * NG:
                        g, half = h // 2, h % 2
                        if half == 0:
                            pe.wait_ge(split_done, NG * n + g + 1)
                        project_half(b, p, g, half)

    @block.scalar
    def _(act):
        from concourse.bass import ds
        chain = Chain(act, act_chain)
        act.sem_inc(raw_done, NG)
        act.sem_inc(split_done, NG)
        act.sem_inc(ssq_done, 1)
        act.sem_inc(ht_lo_done, 1)
        act.sem_inc(y_gated, 1)
        act.sem_inc(y_read, 1)
        act.sem_inc(y_out, 16)
        for s in (*raw_out, *split_out):
            act.sem_inc(s, 16)
        act.wait_ge(consts_in, 64)
        with act.Fori(0, NG) as g:
            for a in range(TPG):
                act.wait_ge(x_loaded[a], 16 * (g + 1))
                act.wait_ge(ssq_done, 1 + TPG * g + a)
                act.activation(w_lo[:, 0].rearrange("p a b -> p (a b)"), x_in[:, a, :], ACT.Square,
                               accum_out=ssq[:, a:a + 1]).then_inc(ssq_done, 1)
            for k in range(KB):
                act.wait_ge(xt_done, KB * g + k + 1)
                act.activation(ht_hi[:, k, ds(g * GRP, GRP)], xbank[k], ACT.Copy,
                               scale=gain[:, k:k + 1]).then_inc(ht_hi_done, 1)

        def tile_in(n):
            act.wait_ge(v_done, n)
            act.wait_ge(tin_done, n + 1)
            act.activation(qkv.rearrange("p h d -> p (h d)"), X[:, 0:6 * P], ACT.Copy).then_inc(qk_out, 1)

        def v_high(n, p):
            act.wait_ge(pv_done, 2 * n)
            act.activation(v_s[:, p, :, 0:HD], v_raw, ACT.Copy).then_inc(v_hi_done, 1)

        def high_parts(n):
            act.wait_ge(rot_done, n + 1)
            act.wait_ge(tk_done, n)
            act.activation(qk_split[:, 0:QK, 0:HALF], rot1, ACT.Copy).then_inc(qs_hi_done, 1)
            act.activation(qk_split[:, 0:QK, HALF:HD], qk[:, :, HALF:HD], ACT.Copy).then_inc(qs_hi_done, 1)

        def swapped_k(n):
            act.wait_ge(qs_lo_done, n + 1)
            act.wait_ge(qs_hi_done, 2 * (n + 1))
            act.activation(qk_split[:, QK:, 0:HD], qk_split[:, SWA_Q:QK, HD:P].bitcast(F32), ACT.Copy)
            act.activation(qk_split[:, QK:, HD:P], qk_split[:, SWA_Q:QK, 0:HD].bitcast(F32),
                           ACT.Copy).then_inc(qs_done, 1)

        def q_out(n):
            act.wait_ge(tq_done, n + 1)
            act.wait_ge(sc_done, 2 * n)
            act.activation(q_t[:, :, :].rearrange("p a b -> p (a b)"), X[:, :], ACT.Copy).then_inc(q_ready, 1)

        def k_out(n, p):
            act.wait_ge(tk_done, n + 1)
            act.activation(k_t[:, :, :, p, :].rearrange("p a b c -> p (a b) c"),
                           X[:, 0:GRP].rearrange("p (a b) -> p a b", a=4), ACT.Copy).then_inc(k_ready, 1)

        def softmax(n, half):
            act.wait_ge(top_done, 2 * n + half + 1)
            for j in range(GQ):
                act.activation(probs[:, j, :], Y[:, j * 2 * P:(j + 1) * 2 * P], ACT.Exp, bias=neg_top[:, j:j + 1],
                               scale=SCALE, accum_out=den[:, j:j + 1])
            act.activation(sink_e[:, :], sink_e[:, :], ACT.Exp).then_inc(exp_done, 1)

        def p_high(n, half):
            act.wait_ge(pt_done, 2 * n + half + 1)
            act.activation(p_hi[:, :], Y[:, :], ACT.Copy).then_inc(p_hi_done, 1)

        def low_values(n, half):
            act.wait_ge(pv_done, 2 * n + half + 1)
            act.activation(y_sum, Y[HD:P, 0:GRP].rearrange("p (a b) -> p a b", a=GQ), ACT.Copy).then_inc(yv_done, 1)

        def raw_group(b, g):
            act.wait_ge(proj_done, NG * b + g + 1)
            act.wait_ge(raw_out[g], 16 + 16 * b)
            act.activation(stage_raw[:, g, :], bank[g][:, :], ACT.Copy).then_inc(raw_done, 1)

        def gate_group(b, g):
            act.wait_ge(proj_done, NG * b + g + 1)
            act.wait_ge(raw_out[g], 16 + 16 * b)
            act.activation(stage_raw[:, g, :], bank[g][:, :], ACT.Sigmoid).then_inc(sigmoid_done, 1)

        with act.Fori(0, GATE_BLOCK // 2) as i:
            for p in range(2):
                for g in range(NG):
                    raw_group(2 * i + p, g)
        act.wait_ge(angles_done, 1)
        act.activation(sin, sin, ACT.Sin).then_inc(rope_done, 1)
        act.activation(cos, cos, ACT.Sin).then_inc(rope_done, 1)
        for p in range(2):
            for g in range(NG):
                gate_group(GATE_BLOCK + p, g)
        b = RAW_BLOCKS - 2
        tile_in(0)
        gate_group(b, 0)
        gate_group(b, 1)
        high_parts(0)
        gate_group(b, 2)
        swapped_k(0)
        gate_group(b, 3)
        q_out(0)
        gate_group(b + 1, 0)
        k_out(0, 0)
        v_high(0, 0)
        for g in range(1, NG):
            gate_group(b + 1, g)
        for g in range(NG):
            act.wait_ge(raw_out[g], 16 * (RAW_BLOCKS + 1))

        with act.Fori(0, NT // 2) as i:
            for p in range(2):
                n = 2 * i + p

                def block_high(g):
                    act.wait_ge(proj_done, NG * (n + RAW_BLOCKS) + g + 1)
                    act.wait_ge(split_out[g % 2], 16 + 32 * (2 * n + g // 2))
                    act.activation(stage_hi[:, g % 2, :], bank[g][:, :], ACT.Copy).then_inc(hi_done, 1)

                tile_in(n + 1)
                softmax(n, 0)
                block_high(0)
                p_high(n, 0)
                high_parts(n + 1)
                low_values(n, 0)
                block_high(1)
                swapped_k(n + 1)
                softmax(n, 1)
                block_high(2)
                q_out(n + 1)
                p_high(n, 1)
                k_out(n + 1, 1 - p)
                low_values(n, 1)
                block_high(3)
                v_high(n + 1, 1 - p)

    @block.vector
    def _(dve):
        from concourse.bass import ds
        chain = Chain(dve, dve_chain)
        dve.wait_ge(consts_in, 64)
        norm_turn = 4
        with dve.Fori(0, NG) as g:
            chain.enter(g, norm_turn)
            dve.wait_ge(ssq_done, 1 + TPG * (g + 1))
            dve.tensor_scalar(ms[:, 0:TPG], ssq[:, 0:TPG], 1.0 / D_MODEL, EPS, ALU.mult, ALU.add).then_inc(ms_done, 1)
            dve.wait_ge(pow_done, g + 1)
            newton_rsqrt(dve, chain, rs[:, 0:TPG], ms[:, 0:TPG], rtmp[:, 0:TPG])
            for a in range(TPG):
                dve.tensor_scalar(x_in[:, a, :], x_in[:, a, :], rs[:, a:a + 1], None, ALU.mult).then_inc(x_scaled, 1)
            for k in range(KB):
                dve.wait_ge(ht_hi_done, KB * g + k + 1)
                at = ds(g * GRP, GRP)
                dve.scalar_tensor_tensor(ht_lo[:, k, at], xbank[k], gain[:, k:k + 1], ht_hi[:, k, at].bitcast(F32),
                                         ALU.mult, ALU.subtract).then_inc(ht_lo_done, 1)
        chain.leave(NG)

        ang, turns, tmp = rope_tmp
        flat = lambda v: v.rearrange("p a b -> p (a b)")
        dve.wait_ge(pos_in, 16)
        dve.wait_ge(consts_made, 2)
        chain.link(dve.tensor_copy(pos[:, :], pos_i[:, :]))
        dve.wait_ge(xt_done, KB * NG)
        dve.wait_ge(x_scaled, TPG * NG)
        chain.link(dve.tensor_tensor(ang, spread(pos[:, :], HALF, 2), spread(inv_freq[:, :], NT, 1), ALU.mult))
        for whole in (4096.0, 1.0):
            chain.link(dve.tensor_scalar(flat(turns), flat(ang), 1.0 / (2 * np.pi * whole), ROUND, ALU.mult, ALU.add))
            chain.link(dve.tensor_scalar(flat(turns), flat(turns), -ROUND, None, ALU.add))
            for part in TWO_PI_PARTS:
                chain.link(dve.scalar_tensor_tensor(flat(ang), flat(turns), -part * whole, flat(ang), ALU.mult, ALU.add))
        chain.link(dve.tensor_scalar(flat(sin), flat(ang), PI, -PI, ALU.min, ALU.max))
        chain.link(dve.tensor_scalar(flat(cos), flat(ang), np.pi / 2, None, ALU.add))
        chain.link(dve.tensor_scalar(flat(tmp), flat(cos), PI, -2 * np.pi, ALU.is_gt, ALU.mult))
        chain.link(dve.tensor_tensor(flat(cos), flat(cos), flat(tmp), ALU.add))
        dve.tensor_scalar(flat(cos), flat(cos), PI, -PI, ALU.min, ALU.max).then_inc(angles_done, 1)

        def gate_groups(m):
            for g in range(NG):
                dve.wait_ge(sigmoid_done, NG * m + g + 1)
                dve.tensor_tensor(stage_raw[:, g, :], bank[g][:, :], stage_raw[:, g, :], ALU.mult).then_inc(raw_done, 1)

        def v_low(n, p):
            dve.wait_ge(v_hi_done, n + 1)
            dve.tensor_tensor(v_s[:, p, :, HD:P], v_raw, v_s[:, p, :, 0:HD].bitcast(F32),
                              ALU.subtract).then_inc(v_done, 1)

        def head_squares(n):
            dve.wait_ge(qk_out, n + 1)
            rot_all = rot.rearrange("p a (h d) -> p (a h) d", d=HD)
            chain.link(dve.tensor_tensor(rot_all, qk, qk, ALU.mult))
            chain.link(dve.tensor_reduce(ssq[:, :], rot_all, AX.X, ALU.add))
            dve.tensor_scalar(ms[:, :], ssq[:, :], 1.0 / HD, EPS, ALU.mult, ALU.add).then_inc(ms_done, 1)

        def norm(n):
            dve.wait_ge(pow_done, NG + n + 1)
            newton_rsqrt(dve, chain, rs[:, :], ms[:, :], rtmp[:, :])
            chain.link(dve.tensor_tensor(qk, qk, spread(rs[:, :], HD, 2), ALU.mult))
            dve.tensor_tensor(qk[:, 0:SWA_Q, :], qk[:, 0:SWA_Q, :], spread(qk_gain[:, 0, :], SWA_Q, 1), ALU.mult)
            chain.link(dve.tensor_tensor(qk[:, SWA_Q:, :], qk[:, SWA_Q:, :], spread(qk_gain[:, 1, :], SWA_KV, 1),
                                         ALU.mult))

        def rotate(tile):
            c_t = spread(cos[:, tile, :], QK, 1)
            s_t = spread(sin[:, tile, :], QK, 1)
            x1, x2 = qk[:, :, 0:HALF], qk[:, :, HALF:HD]
            dve.tensor_tensor(rot1, x1, c_t, ALU.mult)
            chain.link(dve.tensor_tensor(rot2, x2, s_t, ALU.mult))
            chain.link(dve.tensor_tensor(rot1, rot1, rot2, ALU.subtract))
            dve.tensor_tensor(x2, x2, c_t, ALU.mult)
            chain.link(dve.tensor_tensor(rot2, x1, s_t, ALU.mult))
            dve.tensor_tensor(x2, x2, rot2, ALU.add).then_inc(rot_done, 1)

        def low_parts(n):
            dve.wait_ge(qs_hi_done, 2 * (n + 1))
            dve.wait_ge(rot_done, n + 1)
            dve.tensor_tensor(qk_split[:, 0:QK, HD:HD + HALF], rot1, qk_split[:, 0:QK, 0:HALF].bitcast(F32), ALU.subtract)
            dve.tensor_tensor(qk_split[:, 0:QK, HD + HALF:P], qk[:, :, HALF:HD],
                              qk_split[:, 0:QK, HALF:HD].bitcast(F32), ALU.subtract).then_inc(qs_lo_done, 1)

        def top_score(n, half):
            dve.wait_ge(sc_done, 2 * n + half + 1)
            sinks = sink[:, GQ * half:GQ * half + GQ]
            chain.link(dve.tensor_reduce(top[:, :], Y[:, :].rearrange("p (a b) -> p a b", a=GQ), AX.X, ALU.max))
            chain.link(dve.scalar_tensor_tensor(top[:, :], top[:, :], SCALE, sinks, ALU.mult, ALU.max))
            dve.tensor_scalar(neg_top[:, :], top[:, :], -1.0, None, ALU.mult)
            dve.tensor_tensor(sink_e[:, :], sinks, top[:, :], ALU.subtract).then_inc(top_done, 1)

        def normalise(n, half):
            dve.wait_ge(exp_done, 2 * n + half + 1)
            chain.link(dve.tensor_tensor(den[:, :], den[:, :], sink_e[:, :], ALU.add))
            chain.link(dve.reciprocal(den[:, :], den[:, :]))
            dve.tensor_tensor(probs, probs, spread(den[:, :], 2 * P, 2), ALU.mult).then_inc(p_done, 1)

        def p_low(n, half):
            dve.wait_ge(p_hi_done, 2 * n + half + 1)
            dve.tensor_tensor(p_lo[:, :], Y[:, :], p_hi[:, :].bitcast(F32), ALU.subtract).then_inc(p_split, 1)

        def weighted(n, half):
            dve.wait_ge(yv_done, 2 * n + half + 1)
            dve.tensor_tensor(y_sum, y_sum, Y[0:HD, 0:GRP].rearrange("p (a b) -> p a b", a=GQ),
                              ALU.add).then_inc(y_read, 1)
            dve.wait_ge(y_read, 1 + 2 * n + half + 1)
            dve.wait_ge(gate_in, 16 * (n + 1))
            gates = gate_t[:, GQ * half:GQ * half + GQ, :]
            dve.tensor_tensor(gates, y_sum, gates, ALU.mult).then_inc(y_gated, 1)

        gate_groups(0)
        gate_groups(1)
        dve.wait_ge(rope_done, 2)
        head_squares(0)
        norm(0)
        rotate(0)
        low_parts(0)
        gate_groups(2)
        v_low(0, 0)
        gate_groups(3)
        with dve.Fori(0, NT // 2) as i:
            chain.enter(i, 2 * SWA_TURN)
            for p in range(2):
                n = 2 * i + p
                nxt = (n + 1) % NT

                def block_low(g):
                    dve.wait_ge(hi_done, NG * n + g + 1)
                    dve.tensor_tensor(stage_lo[:, g % 2, :], bank[g][:, :], stage_hi[:, g % 2, :].bitcast(F32),
                                      ALU.subtract).then_inc(split_done, 1)

                head_squares(n + 1)
                top_score(n, 0)
                norm(n + 1)
                normalise(n, 0)
                block_low(0)
                rotate(nxt)
                p_low(n, 0)
                low_parts(n + 1)
                weighted(n, 0)
                block_low(1)
                top_score(n, 1)
                normalise(n, 1)
                block_low(2)
                p_low(n, 1)
                weighted(n, 1)
                block_low(3)
                v_low(n + 1, 1 - p)
        chain.leave(NT // 2)


SWA_TURN = 19


PAIRS = SEQ // (2 * P)
TURNS = SB_H // 2
W_SLOTS = 4


class Sticks:

    UNITS = 2 * PAIRS
    V_TURN = 2 * NT // 4

    def __init__(self):
        self.pieces, self.chunk0 = {}, {}
        z = k = 0
        for n in range(self.UNITS):
            j = self.unit(n)[1]
            self.pieces[n] = [(z + m, *cut) for m, cut in enumerate(self.cuts(j))]
            self.chunk0[n] = k
            z, k = z + len(self.pieces[n]), k + j + 1
        self.Z_TURN, self.K_TURN, self.T_TURN = z, k, k + self.V_TURN
        self.pieces[self.UNITS] = [(z + first, *cut) for first, *cut in self.pieces[0]]
        assert z % Z_BANKS == 0 and k % WT_SLOTS == 0 and self.T_TURN % 2 == 0

    @staticmethod
    def unit(n):
        return (0, PAIRS - 1 - n) if n < PAIRS else (1, n - PAIRS) if n < 2 * PAIRS else (0, PAIRS - 1)

    @staticmethod
    def cuts(j):
        ends = [P * (2 * j + 1), P * (2 * j + 2)]
        return [(s, k0, min(GRP, ends[s] - k0)) for k0 in range(ends[1] // GRP * GRP, -1, -GRP)
                for s in range(2) if k0 < ends[s]]

    def order(self, more):
        out, x = [], 0
        for n in range(self.UNITS):
            slot, j = self.unit(n)
            pieces = self.pieces[n + 1] if more or n + 1 < self.UNITS else []
            for c in range(j + 1):
                out += [("piece", n + 1, q) for m, q in enumerate(pieces) if m * (j + 1) // len(pieces) == c]
                out.append(("chunk", self.chunk0[n] + c, n, j - c, x))
                x += 1
                if j == PAIRS - 3 and 1 <= c <= NT // 4 and (slot == 0 or more):
                    out.append(("v", 1 - slot, c - 1, x))
                    x += 1
        return out

    def needed(self, n, m):
        return max(z for z, _, k0, _ in self.pieces[n] if k0 == 2 * m * P // GRP * GRP)

    def last_chunk(self, n):
        return self.chunk0[n] + self.unit(n)[1]


Z_BANKS, WT_SLOTS = 4, 3
V_AT = 3


def sticks(nc, c, t, wo):
    from concourse.bass import ds
    o = Sticks()
    sb = lambda n, s, d=F32: c.enter_context(nc.sbuf_tensor(n, s, d))
    sem = lambda n: c.enter_context(nc.semaphore(n))
    q_s = sb("q_s", [P, 2, SEQ], F32R)
    k_s = sb("k_s", [P, 2, 2, SEQ], F32R)
    v_t = sb("v_t", [P, SEQ])
    v_s = sb("vb_s", [P, 2, NT, P])
    take = sb("take", [P, 4, SEQ])
    left = sb("left", [P, 4, SEQ])
    wt = sb("wt", [P, WT_SLOTS, 4 * P])
    gate_hi, gate_lo, gate = sb("gate_hi", [P, SEQ]), sb("gate_lo", [P, SEQ]), sb("gate", [P, SEQ])
    y = sb("yb", [P, SEQ])
    ident, ident_bf = sb("identb", [P, P]), sb("identb_bf", [P, P], BF16)
    twice = sb("twice", [P, P])
    mask = sb("mask", [P, P], BF16)
    Z = [c.enter_context(nc.psum_tensor(f"Z{s}", [P, GRP], F32)) for s in range(Z_BANKS)]
    T = [c.enter_context(nc.psum_tensor(f"T{s}", [P, 4 * P], F32)) for s in range(2)]
    O = [c.enter_context(nc.psum_tensor(f"O{s}", [P, 4 * P], F32)) for s in range(2)]
    consts, chain_sem = sem("b_consts"), sem("b_chain")
    late_in = sem("late_in")
    head_in = [sem(f"head_in{p}") for p in range(2)]
    v_in, gate_in, gate_sum, gate_sig, gate_done = (sem(n) for n in (
        "v_in", "b_gate_in", "gate_sum", "gate_sig", "gate_done"))
    z_done, z_read, scanned, w_done = sem("z_done"), sem("z_read"), sem("scanned"), sem("w_done")
    t_done, t_read, pv_done, gated = sem("t_done"), sem("t_read"), sem("b_pv_done"), sem("gated")
    y_out = [sem(f"b_y_out{s}") for s in range(2)]
    Z0, PV0, O0 = Z_BANKS, WT_SLOTS, 2
    T0 = NT // 4
    HB = SB_H * HD
    QK_LOADS = 6

    block = c.enter_context(nc.Block())

    @block.sync
    def _(sp):
        def rows(name, kind, head):
            return t[name][ds(kind * HB + head * HD, HD), :]

        def load_qk(head, p, done, at=slice(0, SEQ)):
            for half, (first, second) in enumerate((("hi", "lo"), ("lo", "hi"))):
                to = slice(half * HD, half * HD + HD)
                sp.dma_start(q_s[to, p, at].bitcast(F32), rows(first, 0, head)[:, at]).then_inc(done, 16)
                sp.dma_start(k_s[to, p, 0, at].bitcast(F32), rows(first, 1, head)[:, at]).then_inc(done, 16)
                sp.dma_start(k_s[to, p, 1, at].bitcast(F32), rows(second, 1, head)[:, at]).then_inc(done, 16)

        def load_v(head):
            for half, name in enumerate(("hi", "lo")):
                sp.dma_start(v_t[half * HD:half * HD + HD, :], rows(name, 2, head)).then_inc(v_in, 16)

        def load_gate(pair):
            sp.dma_start(gate_hi[:, :], t["hi"][ds(3 * HB + pair * P, P), :]).then_inc(gate_in, 16)
            sp.dma_start(gate_lo[:, :], t["lo"][ds(3 * HB + pair * P, P), :]).then_inc(gate_in, 16)

        def turn(i, more):
            if more:
                sp.wait_ge(gate_done, i + 1)
                load_gate(i + 1)
            v_last = [max(step[3] for step in o.order(True) if step[0] == "v" and step[1] == p) for p in range(2)]
            for p in range(2):
                last = o.pieces[PAIRS * (p + 1) - 1][-1][0]
                if more:
                    sp.wait_ge(t_done, T0 + o.T_TURN * i + v_last[1 - p] + 1)
                    load_v(2 * i + 2 + p)
                    sp.wait_ge(z_done, o.Z_TURN * i + last + 1)
                    load_qk(2 * i + 2 + p, p, head_in[p])
                sp.wait_ge(gated, O0 + o.UNITS * i + PAIRS * (p + 1))
                sp.dma_start(t["y"][ds(SWA_Q * HD + i * P + p * HD, HD), :],
                             y[p * HD:p * HD + HD, :]).then_inc(y_out[p], 16)

        load_qk(0, 0, late_in, slice(SEQ // 2, SEQ))
        load_v(0)
        load_qk(0, 0, head_in[0], slice(0, SEQ // 2))
        load_gate(0)
        load_qk(1, 1, head_in[1])
        sp.wait_ge(t_done, T0)
        load_v(1)
        with sp.Fori(0, TURNS - 1) as i:
            turn(i, True)
        for k in range(W_SLOTS):
            sp.dma_start(wo.raw[:, k, :], wo.view[:, k, :]).then_inc(wo.loaded[k], 16)
        turn(TURNS - 1, False)
        for s in range(2):
            sp.wait_ge(y_out[s], 16 * (TURNS + 1))

    @block.gpsimd
    def _(pool):
        chain = Chain(pool, chain_sem)
        diagonal = lambda m, base: chain.link(pool.affine_select(
            out=m, in_=m, compare_op=ALU.not_equal, fill=1.0, base=base, pattern=[[-1, P]], channel_multiplier=1))
        chain.link(pool.memset(ident[:, :], 0.0))
        diagonal(ident[:, :], 0)
        chain.link(pool.tensor_copy(ident_bf[:, :], ident[:, :]))
        chain.link(pool.memset(mask[:, :], 0.0))
        chain.link(pool.memset(twice[:, :], 0.0))
        for base in (0, HD, -HD):
            diagonal(twice[:, :], base)
        pool.affine_select(out=mask[:, :], in_=mask[:, :], compare_op=ALU.is_gt, fill=MASKED, base=0,
                           pattern=[[-1, P]], channel_multiplier=1).then_inc(consts, 1)

    @block.tensor
    def _(pe):
        mm = pe.matmul

        def scores(i, n, piece):
            z, s, k0, keys = piece
            p, j = o.unit(n)
            a = 2 * j + s
            out = Z[z % Z_BANKS]
            pe.wait_ge(z_read, Z0 + o.Z_TURN * i + z - Z_BANKS + 1)
            last = k0 + keys == P * (a + 1)
            for part in range(2):
                ins = mm(out[:, 0:keys], q_s[:, p, a * P:(a + 1) * P],
                         k_s[:, p, part, k0:k0 + keys], start=part == 0, stop=part == 1 and not last)
            if last:
                ins = mm(out[:, keys - P:keys], ident_bf[:, :], mask[:, :], start=False, stop=True)
            ins.then_inc(z_done, 1)

        def columns_v(i, p, m, x):
            if x >= 2 - T0:
                pe.wait_ge(t_read, T0 + o.T_TURN * i + x - 1)
            for b in range(4):
                ins = mm(T[x % 2][:, b * P:(b + 1) * P], v_t[:, (4 * m + b) * P:(4 * m + b + 1) * P],
                         twice[:, :], start=True, stop=True)
            ins.then_inc(t_done, 1)

        def transpose_w(i, n, m, x):
            pe.wait_ge(t_read, T0 + o.T_TURN * i + x - 1)
            blocks = [(2 * m, 0), (2 * m, 1), (2 * m + 1, 0), (2 * m + 1, 1)]
            if m == o.unit(n)[1]:
                blocks.remove((2 * m + 1, 0))
            pe.wait_ge(w_done, o.Z_TURN * i + o.needed(n, m) + 1)
            for b, (kb, s) in enumerate(blocks):
                ins = pe.transpose(T[x % 2][:, b * P:(b + 1) * P], take[:, (2 * n + s) % 4, kb * P:(kb + 1) * P],
                                   ident[:, :])
            ins.then_inc(t_done, 1)

        def values(i, k, n, m, x):
            p, j = o.unit(n)
            pe.wait_ge(t_read, T0 + o.T_TURN * i + x + 1)
            if m == j:
                pe.wait_ge(gated, O0 + o.UNITS * i + n - 1)
            for b in range(2):
                at, first = (2 * P, P) if m == j and b else (b * 2 * P, 0)
                ins = mm(O[n % 2][:, first:2 * P], v_s[:, p, 2 * m + b, :], wt[:, k % WT_SLOTS, at:at + 2 * P - first],
                         start=m == j and b == 0, stop=m == 0 and b == 1)
            ins.then_inc(pv_done, 1)

        def turn(i, more):
            waiting = []
            for kind, *step in o.order(more):
                if kind == "piece":
                    if step[0] == PAIRS and step[1] == o.pieces[PAIRS][0]:
                        pe.wait_ge(head_in[1], 16 * QK_LOADS * (i + 1))
                    if step[0] == o.UNITS and step[1] == o.pieces[o.UNITS][0]:
                        pe.wait_ge(head_in[0], 16 * QK_LOADS * (i + 2))
                    scores(i, *step)
                elif kind == "v":
                    slot, m, x = step
                    if m == 0:
                        pe.wait_ge(v_in, 32 * (2 * i + 3 - slot))
                    columns_v(i, slot, m, x)
                else:
                    k, n, m, x = step
                    transpose_w(i, n, m, x)
                    waiting.append(step)
                    if len(waiting) == WT_SLOTS:
                        values(i, *waiting.pop(0))
            for chunk in waiting:
                values(i, *chunk)

        pe.wait_ge(consts, 1)
        pe.wait_ge(late_in, 16 * QK_LOADS)
        for n, piece in enumerate(o.pieces[0]):
            if n == V_AT:
                pe.wait_ge(v_in, 32)
                for m in range(T0):
                    columns_v(0, 0, m, m - T0)
            if piece[2] + GRP == SEQ // 2 and piece[1] == 0:
                pe.wait_ge(head_in[0], 16 * QK_LOADS)
            scores(0, 0, piece)
        with pe.Fori(0, TURNS - 1) as i:
            turn(i, True)
        turn(TURNS - 1, False)

    @block.scalar
    def _(act):
        act.sem_inc(z_read, Z0)
        act.sem_inc(pv_done, PV0)
        act.sem_inc(gated, O0)
        for s in range(2):
            act.sem_inc(y_out[s], 16)

        def sigmoids(i, n, piece, x_last=None):
            z, s, k0, keys = piece
            tile = (2 * n + s) % 4
            if n and piece == o.pieces[n][0]:
                before = x_last[n - 2] + 1 if n > 1 else 0
                act.wait_ge(t_done, T0 + o.T_TURN * i + before)
            act.wait_ge(z_done, o.Z_TURN * i + z + 1)
            bank = Z[z % Z_BANKS][:, 0:keys]
            act.activation(left[:, tile, k0:k0 + keys], bank, ACT.Sigmoid, scale=-SCALE)
            act.activation(take[:, tile, k0:k0 + keys], bank, ACT.Sigmoid, scale=SCALE).then_inc(z_read, 1)

        def copy_v(i, p, m, x):
            act.wait_ge(t_done, T0 + o.T_TURN * i + x + 1)
            act.activation(v_s[:, p, 4 * m:4 * m + 4, :].rearrange("p a b -> p (a b)"), T[x % 2][:, :],
                           ACT.Copy).then_inc(t_read, 1)

        def copy_w(i, k, n, m, x):
            w = 3 * P if m == o.unit(n)[1] else 4 * P
            act.wait_ge(t_done, T0 + o.T_TURN * i + x + 1)
            act.wait_ge(pv_done, PV0 + o.K_TURN * i + k - WT_SLOTS + 1)
            act.activation(wt[:, k % WT_SLOTS, 0:w], T[x % 2][:, 0:w], ACT.Copy).then_inc(t_read, 1)

        def turn(i, more):
            x_last = {}
            for kind, *step in o.order(more):
                if kind == "piece":
                    sigmoids(i, *step, x_last)
                elif kind == "v":
                    if step[1] == 0:
                        act.wait_ge(pv_done, PV0 + o.K_TURN * i + (0 if step[0] else o.chunk0[PAIRS]))
                    copy_v(i, *step)
                else:
                    copy_w(i, *step)
                    x_last[step[1]] = step[3]
                    if step[0] == GATE_STEPS[1]:
                        act.wait_ge(gate_sum, i + 1)
                        act.activation(gate_lo[:, :], gate[:, :], ACT.Sigmoid).then_inc(gate_sig, 1)

        for n, piece in enumerate(o.pieces[0]):
            if n == V_AT:
                for m in range(T0):
                    copy_v(0, 0, m, m - T0)
            sigmoids(0, 0, piece)
        with act.Fori(0, TURNS - 1) as i:
            turn(i, True)
        turn(TURNS - 1, False)

    @block.vector
    def _(dve):
        def products(i, n, piece):
            z, s, k0, keys = piece
            tile = (2 * n + s) % 4
            at = left[:, tile, k0:k0 + keys][:, ::-1]
            first = k0 + keys == P * (2 * o.unit(n)[1] + s + 1)
            dve.wait_ge(z_read, Z0 + o.Z_TURN * i + z + 1)
            if not first:
                before = max(b for b, s1, _, _ in o.pieces[n] if s1 == s and b < z)
                dve.wait_ge(scanned, o.Z_TURN * i + before + 1)
            dve.tensor_tensor_scan(at, at, at, 1.0 if first else left[:, tile, k0 + keys:k0 + keys + 1],
                                   ALU.mult, ALU.min).then_inc(scanned, 1)

        def weights(i, n, piece):
            z, s, k0, keys = piece
            tile = (2 * n + s) % 4
            if k0 + keys == P * (2 * o.unit(n)[1] + s + 1):
                keys -= 1
            dve.wait_ge(scanned, o.Z_TURN * i + z + 1)
            at = take[:, tile, k0:k0 + keys]
            dve.tensor_tensor(at, at, left[:, tile, k0 + 1:k0 + keys + 1], ALU.mult).then_inc(w_done, 1)

        def gate_sums(i, n):
            p, j = o.unit(n)
            at, cols = slice(p * HD, p * HD + HD), slice(j * 2 * P, (j + 1) * 2 * P)
            dve.wait_ge(pv_done, PV0 + o.K_TURN * i + o.last_chunk(n) + 1)
            if n % PAIRS == 0:
                dve.wait_ge(y_out[p], 16 * (i + 1))
            dve.tensor_tensor(y[at, cols], O[n % 2][at, 0:2 * P], gate[at, cols], ALU.mult).then_inc(gated, 1)

        def turn(i, more):
            multiplied = (0, o.pieces[0][-1])
            for kind, *step in o.order(more):
                if kind == "piece":
                    products(i, *step)
                    weights(i, *multiplied)
                    multiplied = step
                elif kind == "chunk":
                    k, n, m, x = step
                    if k == GATE_STEPS[0]:
                        dve.wait_ge(gate_in, 32 * (i + 1))
                        dve.tensor_tensor(gate[:, :], gate_hi[:, :], gate_lo[:, :], ALU.add).then_inc(gate_sum, 1)
                    if k == GATE_STEPS[2]:
                        dve.wait_ge(gate_sig, i + 1)
                        dve.tensor_tensor(gate[:, :], gate[:, :], gate_lo[:, :], ALU.mult).then_inc(gate_done, 1)
                        dve.wait_ge(gate_done, i + 1)
                    for n in range(o.UNITS - 1):
                        if k == o.last_chunk(n) + WT_SLOTS:
                            gate_sums(i, n)
                    if not more and k == o.chunk0[o.UNITS - 1]:
                        weights(i, *multiplied)
            gate_sums(i, o.UNITS - 1)

        for n, piece in enumerate(o.pieces[0]):
            products(0, 0, piece)
            if n:
                weights(0, 0, o.pieces[0][n - 1])
        with dve.Fori(0, TURNS - 1) as i:
            turn(i, True)
        turn(TURNS - 1, False)


GATE_STEPS = (3, 5, 8)


class WOut:

    def __init__(self, nc, c, t):
        self.raw = c.enter_context(nc.sbuf_tensor("wo_raw", [P, W_SLOTS, D_MODEL], F32))
        self.loaded = [c.enter_context(nc.semaphore(f"wo_loaded{s}")) for s in range(W_SLOTS)]
        self.view = t["w_out"].rearrange("l (k p) n -> p (l k) n", p=P)


def mix_out(nc, c, t, wo):
    from concourse.bass import ds
    sb = lambda n, s, d=F32: c.enter_context(nc.sbuf_tensor(n, s, d))
    sem = lambda n: c.enter_context(nc.semaphore(n))
    w_hi, w_lo = sb("wo_hi", [P, KB, D_MODEL], F32R), sb("wo_lo", [P, KB, D_MODEL], F32R)
    y_raw = sb("y_raw", [P, TPG, KB, P])
    y_hi, y_lo = sb("yo_hi", [P, TPG, KB, P], F32R), sb("yo_lo", [P, TPG, KB, P], F32R)
    x_t, out_t = sb("x_t", [P, TPG, D_MODEL]), sb("out_t", [P, TPG, D_MODEL])
    HALVES = D_MODEL // GRP
    bank = [c.enter_context(nc.psum_tensor(f"obank{n}", [P, GRP], F32)) for n in range(TPG * HALVES)]
    w_hi_done, w_split = sem("wo_hi_done"), sem("wo_split")
    y_in, x_in, out_out = ([sem(f"{n}{s}") for s in range(TPG)] for n in ("yo_in", "xo_in", "out_out"))
    y_hi_done, y_split = sem("yo_hi_done"), sem("yo_split")
    tile_done, out_done = sem("tile_done"), sem("out_done")
    block = c.enter_context(nc.Block())
    y_view = t["y"].rearrange("(k p) t -> p k t", p=P)

    @block.sync
    def _(sp):
        def load_y(tile, s):
            sp.dma_start(y_raw[:, s], y_view[:, :, ds(tile * P, P)]).then_inc(y_in[s], 16)

        def load_x(tile, s):
            sp.dma_start(x_t[:, s, :], t["x"][0, ds(tile * P, P), :]).then_inc(x_in[s], 16)

        def store(tile, s):
            sp.wait_ge(out_done, HALVES * (tile + TPG + 1))
            sp.dma_start(t["out"][0, ds(tile * P, P), :], out_t[:, s, :]).then_inc(out_out[s], 16)

        for s in range(TPG):
            load_y(s, s)
        for k in range(W_SLOTS, KB):
            sp.wait_ge(w_split, k - W_SLOTS + 1)
            sp.dma_start(wo.raw[:, k % W_SLOTS, :], wo.view[:, k, :]).then_inc(wo.loaded[k % W_SLOTS], 16)
        for s in range(TPG):
            load_x(s, s)
        with sp.Fori(0, NG - 1) as g:
            for s in range(TPG):
                sp.wait_ge(y_split, TPG * g + s + 1)
                load_y(TPG * (g + 1) + s, s)
            for s in range(TPG):
                store(TPG * g + s, s)
                load_x(TPG * (g + 1) + s, s)
        for s in range(TPG):
            store(TPG * (NG - 1) + s, s)
        for s in range(TPG):
            sp.wait_ge(out_out[s], 16 * (NG + 1))

    @block.scalar
    def _(act):
        def w_high(k):
            act.wait_ge(wo.loaded[k % W_SLOTS], 16 * (k // W_SLOTS + 1))
            act.activation(w_hi[:, k, :], wo.raw[:, k % W_SLOTS, :], ACT.Copy).then_inc(w_hi_done, 1)

        def y_high(g, s):
            act.wait_ge(y_in[s], 16 * (g + 1))
            act.wait_ge(tile_done, HALVES * (TPG * g + s + 1))
            act.activation(y_hi[:, s], y_raw[:, s], ACT.Copy).then_inc(y_hi_done, 1)

        act.sem_inc(tile_done, HALVES * TPG)
        act.sem_inc(out_done, HALVES * TPG)
        for s in range(TPG):
            act.sem_inc(out_out[s], 16)
        for k in range(KB):
            w_high(k)
            if k == 1:
                for s in range(TPG):
                    y_high(0, s)
        with act.Fori(1, NG) as g:
            for s in range(TPG):
                y_high(g, s)

    @block.tensor
    def _(pe):
        passes = ((y_hi, w_hi), (y_hi, w_lo), (y_lo, w_hi))

        def product(s, h, k, n):
            y_part, w_part = passes[n]
            return pe.matmul(bank[HALVES * s + h][:, :], y_part[:, s, k, :], w_part[:, k, h * GRP:(h + 1) * GRP],
                             start=k == 0 and n == 0, stop=k == KB - 1 and n == len(passes) - 1)

        for k in range(KB):
            pe.wait_ge(w_split, k + 1)
            for s in range(TPG):
                if k == 0:
                    pe.wait_ge(y_split, s + 1)
                for h in range(HALVES):
                    for n in range(len(passes)):
                        ins = product(s, h, k, n)
                    if k == KB - 1:
                        ins.then_inc(tile_done, 1)
        with pe.Fori(1, NG) as g:
            for s in range(TPG):
                pe.wait_ge(y_split, TPG * g + s + 1)
                for h in range(HALVES):
                    pe.wait_ge(out_done, HALVES * (TPG * g + s) + h + 1)
                    for k in range(KB):
                        for n in range(len(passes)):
                            ins = product(s, h, k, n)
                    ins.then_inc(tile_done, 1)

    @block.vector
    def _(dve):
        def w_low(k):
            dve.wait_ge(w_hi_done, k + 1)
            dve.tensor_tensor(w_lo[:, k, :], wo.raw[:, k % W_SLOTS, :], w_hi[:, k, :].bitcast(F32),
                              ALU.subtract).then_inc(w_split, 1)

        def y_low(g, s):
            dve.wait_ge(y_hi_done, TPG * g + s + 1)
            dve.tensor_tensor(y_lo[:, s], y_raw[:, s], y_hi[:, s].bitcast(F32), ALU.subtract).then_inc(y_split, 1)

        def add_x(g, s):
            dve.wait_ge(x_in[s], 16 * (g + 1))
            dve.wait_ge(out_out[s], 16 * (g + 1))
            for h in range(HALVES):
                at = slice(h * GRP, (h + 1) * GRP)
                dve.wait_ge(tile_done, HALVES * (TPG * (g + 1) + s) + h + 1)
                dve.tensor_tensor(out_t[:, s, at], bank[HALVES * s + h][:, :], x_t[:, s, at],
                                  ALU.add).then_inc(out_done, 1)

        for k in range(KB):
            w_low(k)
            if k == 1:
                for s in range(TPG):
                    y_low(0, s)
        with dve.Fori(0, NG - 1) as g:
            for s in range(TPG):
                add_x(g, s)
                y_low(g + 1, s)
        for s in range(TPG):
            add_x(NG - 1, s)


def build(nc, t):
    with ExitStack() as c:
        project(nc, c, t)
    with ExitStack() as shared:
        wo = WOut(nc, shared, t)
        for stage in (sticks, mix_out):
            with ExitStack() as c:
                stage(nc, c, t, wo)


def kernel(**inputs):
    import concourse.bacc as bacc
    from concourse.bass_utils import run_bass_kernel_spmd

    nc = bacc.Bacc("TRN2", target_bir_lowering=False, num_devices=1)
    arrays, t = {}, {}
    for name in ("x", "positions", "norm_gain", "w_in", "q_norm_gain", "k_norm_gain", "sinks", "w_out"):
        a = np.ascontiguousarray(inputs[name])
        arrays[f"in_{name}"] = a
        t[name] = nc.dram_tensor(f"in_{name}", a.shape, mybir.dt.from_np(a.dtype), kind="ExternalInput").ap()
    for name, rows in (("raw", RAW_BLOCKS * P), ("hi", SPLIT_BLOCKS * P), ("lo", SPLIT_BLOCKS * P),
                       ("y", D_MODEL)):
        t[name] = nc.dram_tensor(f"scratch_{name}", (rows, SEQ), F32).ap()
    t["out"] = nc.dram_tensor("out", (1, SEQ, D_MODEL), F32, kind="ExternalOutput").ap()
    build(nc, t)
    r = run_bass_kernel_spmd(nc, [arrays], core_ids=[0])
    return r.results[0]["out"]
```

```python
from contextlib import ExitStack

import numpy as np
from concourse import mybir

F32 = mybir.dt.float32
F32R = mybir.dt.float32r
BF16 = mybir.dt.bfloat16
I32 = mybir.dt.int32
ALU = mybir.AluOpType
ACT = mybir.ActivationFunctionType
AX = mybir.AxisListType

P = 128
SEQ, D_MODEL = 2048, 1024
HD = 64
HALF = HD // 2
KB = D_MODEL // P
GRP = 512
NG = SEQ // GRP
NT = SEQ // P
TPG = GRP // P
SWA_Q, SWA_KV, SB_H = 8, 2, 8
GQ = SWA_Q // SWA_KV
RAW_BLOCKS = 10
GATE_BLOCK = 6
SPLIT_BLOCKS = 16
QK = SWA_Q + SWA_KV
EPS = 1e-6
SCALE = HD ** -0.5
MASKED = -1e30
THETA = 10000.0
PI = float(np.float32(3.1415925))
TWO_PI_PARTS = (6.25, 0.033203125, -1.7881393432617188e-05, 2 * np.pi - 6.25 - 0.033203125 + 1.7881393432617188e-05)
ROUND = float(1.5 * 2 ** 23)


def view(buf, at, shape):
    n = int(np.prod(shape))
    v = buf[:, at:at + n]
    if len(shape) == 2:
        v = v.rearrange("p (a b) -> p a b", a=shape[0])
    return v


def spread(ap, n, where):
    shape = list(ap.shape)
    shape.insert(where, n)
    return ap.unsqueeze(where).broadcast_to(shape)


class Chain:

    def __init__(self, eng, sem):
        self.eng, self.sem, self.n, self.turn = eng, sem, 0, 0

    def mark(self, ins):
        ins.then_inc(self.sem, 1)
        self.n += 1

    def wait(self):
        self.eng.wait_ge(self.sem, self.turn + self.n)

    def link(self, ins):
        self.mark(ins)
        self.wait()

    def enter(self, i, per_turn):
        self.turn, self.base, self.per_turn = i * per_turn, self.n, per_turn

    def leave(self, turns):
        assert self.n - self.base == self.per_turn, (self.n - self.base, self.per_turn)
        self.turn, self.n = 0, self.base + turns * self.per_turn


def newton_rsqrt(dve, chain, y, ms, tmp):
    chain.link(dve.tensor_tensor(tmp, y, y, ALU.mult))
    chain.link(dve.tensor_tensor(tmp, tmp, ms, ALU.mult))
    chain.link(dve.tensor_scalar(tmp, tmp, -0.5, 1.5, ALU.mult, ALU.add))
    chain.link(dve.tensor_tensor(y, y, tmp, ALU.mult))


def project(nc, c, t, stores):
    sb = lambda n, s, d=F32: c.enter_context(nc.sbuf_tensor(n, s, d))
    sem = lambda n: c.enter_context(nc.semaphore(n))
    ht_hi, ht_lo = sb("ht_hi", [P, KB, SEQ], F32R), sb("ht_lo", [P, KB, SEQ], F32R)
    w_hi, w_lo = sb("w_hi", [P, 2, KB, P], F32R), sb("w_lo", [P, 2, KB, P], F32R)
    w_raw = sb("w_raw", [P, 2, KB // 2, P])
    arena = sb("arena", [P, 5248])
    x_in = view(arena, 0, (TPG, D_MODEL))
    qkv_t = view(arena, 0, (6, P))
    qkv = view(arena, 768, (QK + SWA_KV, HD))
    qk, v_raw = qkv[:, 0:QK, :], qkv[:, QK:, :]
    rot = view(arena, 1536, (2, QK * HALF))
    rot1, rot2 = (rot[:, n, :].rearrange("p (h d) -> p h d", h=QK) for n in range(2))
    probs = view(arena, 2176, (GQ, 2 * P))
    y_sum = view(arena, 2176, (GQ, P))[0:HD]
    gate_t = view(arena, 3200, (SWA_Q, P))[0:HD]
    stage_raw = view(arena, 2176, (NG, GRP))
    rope_tmp = [view(arena, 512 * n, (NT, HALF)) for n in range(3)]
    gain = arena[:, 4224:4224 + D_MODEL]
    cos, sin = view(arena, 4224, (NT, HALF)), view(arena, 4736, (NT, HALF))
    stage_hi, stage_lo = sb("stage_hi", [P, 2, GRP], F32R), sb("stage_lo", [P, 2, GRP], F32R)
    qk_split = sb("qk_split", [P, QK + SWA_KV, P], F32R)
    q_t = sb("q_t", [P, SWA_Q, P], F32R)
    k_t = sb("k_t", [P, 2, SWA_KV, 2, P], F32R)
    v_s = sb("v_s", [P, 2, SWA_KV, P], F32R)
    p_hi, p_lo = sb("p_hi", [P, 2 * GQ * P], F32R), sb("p_lo", [P, 2 * GQ * P], F32R)
    ident, ident_bf = sb("ident", [P, P]), sb("ident_bf", [P, P], BF16)
    mask_even = sb("mask_even", [P, 2, 2 * P], BF16)
    mask_odd = sb("mask_odd", [P, 2 * P], BF16)
    qk_gain = sb("qk_gain", [P, 2, HD])
    sink = sb("sink", [P, SWA_Q])
    inv_freq = sb("inv_freq", [P, HALF])
    pos_i, pos = sb("pos_i", [P, NT], I32), sb("pos", [P, NT])
    power = sb("power", [P, QK])
    ssq, ms, rs, rtmp = (sb(n, [P, QK]) for n in ("ssq", "ms", "rs", "rtmp"))
    top, neg_top, sink_e, den = (sb(n, [P, GQ]) for n in ("top", "neg_top", "sink_e", "den"))
    A, B, X, Y = (c.enter_context(nc.psum_tensor(n, [P, 2 * GRP], F32)) for n in ("A", "B", "X", "Y"))
    bank = [A[:, 0:GRP], A[:, GRP:], B[:, 0:GRP], B[:, GRP:]]
    x_t = (X, Y)

    x_loaded = [sem(f"x_loaded{a}") for a in range(TPG)]
    consts_in, pos_in, gain_in = sem("consts_in"), sem("pos_in"), sem("gain_in")
    ssq_done, ms_done, pow_done, x_scaled = sem("ssq_done"), sem("ms_done"), sem("pow_done"), sem("x_scaled")
    xt_done, ht_hi_done, ht_lo_done = sem("xt_done"), sem("ht_hi_done"), sem("ht_lo_done")
    pool_chain, dve_chain = sem("pool_chain"), sem("dve_chain")
    consts_made = sem("consts_made")
    w_loaded = [sem(f"w_loaded{h}") for h in range(2)]
    w_hi_done, w_split = sem("w_hi_done"), sem("w_split")
    sigmoid_done = sem("sigmoid_done")
    proj_done, raw_done, hi_done, split_done = sem("proj_done"), sem("raw_done"), sem("hi_done"), sem("split_done")
    raw_out = [sem(f"raw_out{g}") for g in range(NG)]
    split_out, y_out = stores.split_out, stores.y_out
    angles_done, rope_done = sem("angles_done"), sem("rope_done")
    qkv_in, gate_in = sem("qkv_in"), sem("gate_in")
    tin_done, qk_out, v_hi_done, v_done = sem("tin_done"), sem("qk_out"), sem("v_hi_done"), sem("v_done")
    rot_done, qs_hi_done, qs_lo_done, qs_done = sem("rot_done"), sem("qs_hi_done"), sem("qs_lo_done"), sem("qs_done")
    tq_done, q_ready, tk_done, k_ready = sem("tq_done"), sem("q_ready"), sem("tk_done"), sem("k_ready")
    sc_done, top_done, exp_done, p_done = sem("sc_done"), sem("top_done"), sem("exp_done"), sem("p_done")
    pt_done, p_hi_done, p_split = sem("pt_done"), sem("p_hi_done"), sem("p_split")
    pv_done, yv_done, y_read, y_gated = sem("pv_done"), sem("yv_done"), sem("y_read"), sem("y_gated")
    w_seen, y_seen = sem("w_seen"), sem("y_seen")
    block = c.enter_context(nc.Block())

    w_view = t["w_in"].rearrange("l (k p) n -> p (l k) n", p=P)
    raw_view = t["raw"].rearrange("(b p) t -> p b t", p=P)
    gate_view = t["raw"][6 * P:RAW_BLOCKS * P, :].rearrange("(h d) t -> d h t", d=HD)
    y_view = t["y"][0:SWA_Q * HD, :].rearrange("(h d) t -> d h t", d=HD)

    @block.sync
    def _(sp):
        from concourse.bass import ds

        def load_x(a, tile):
            sp.dma_start(x_in[:, a, :], t["x"][0, ds(tile * P, P), :]).then_inc(x_loaded[a], 16)

        def load_w(b):
            for h in range(2):
                sp.dma_start(w_raw[:, h], w_view[:, 4 * h:4 * h + 4, ds(b * P, P)]).then_inc(w_loaded[h], 16)

        def prefetch_w(b):
            for h in range(2):
                sp.wait_ge(w_split, 2 * b + h + 1)
                sp.dma_start(w_raw[:, h], w_view[:, 4 * h:4 * h + 4, ds((b + 1) * P, P)]).then_inc(w_loaded[h], 16)

        for a in range(TPG):
            load_x(a, a)
            if a == 0:
                sp.dma_start(gain, t["norm_gain"].broadcast_to([P, D_MODEL])).then_inc(gain_in, 16)
        with nc.allow_non_contiguous_dma(reason="small columns of constants"):
            sp.dma_start(pos_i[:, :], t["positions"].rearrange("b (n p) -> p (b n)", p=P)).then_inc(pos_in, 16)
        sp.dma_start(qk_gain[:, 0, :], t["q_norm_gain"].broadcast_to([P, HD])).then_inc(consts_in, 16)
        sp.dma_start(qk_gain[:, 1, :], t["k_norm_gain"].broadcast_to([P, HD])).then_inc(consts_in, 16)
        sp.dma_start(sink[:, :], t["sinks"].broadcast_to([P, SWA_Q])).then_inc(consts_in, 16)
        load_w(0)
        with sp.Fori(1, NG) as g:
            for a in range(TPG):
                sp.wait_ge(xt_done, TPG * (g - 1) + a + 1)
                load_x(a, TPG * g + a)

        def raw_block(b):
            prefetch_w(b)
            for g in range(NG):
                sp.wait_ge(raw_done, NG + NG * b + g + 1)
                sp.dma_start(t["raw"][ds(b * P, P), g * GRP:(g + 1) * GRP],
                             stage_raw[:, g, :]).then_inc(raw_out[g], 16)

        with sp.Fori(0, GATE_BLOCK // 2) as i:
            for p in range(2):
                raw_block(2 * i + p)

        def load_qkv(tile, n):
            sp.wait_ge(tin_done, n)
            sp.dma_start(qkv_t, raw_view[:, 0:6, ds(tile * P, P)]).then_inc(qkv_in, 16)

        def store_y(tile, half):
            n = 2 * tile + half
            sp.wait_ge(y_gated, 1 + n + 1)
            sp.sem_inc(y_seen, 1)
            sp.dma_start(y_view[:, GQ * half:GQ * half + GQ, ds(tile * P, P)],
                         gate_t[:, GQ * half:GQ * half + GQ, :]).then_inc(y_out, 16)

        def split_block(tile, more):
            if more:
                nxt = sp.snap((tile + 2) % NT)
                load_qkv(nxt, tile + 2)
                prefetch_w(tile + RAW_BLOCKS)
            sp.wait_ge(y_out, 16 + 16 * 2 * tile)
            sp.dma_start(gate_t, gate_view[:, :, ds(tile * P, P)]).then_inc(gate_in, 16)
            for g in range(NG):
                sp.wait_ge(split_done, NG + NG * tile + g + 1)
                for st, d in ((stage_hi, "hi"), (stage_lo, "lo")):
                    sp.dma_start(t[d][ds(tile * P, P), g * GRP:(g + 1) * GRP],
                                 st[:, g % 2, :].bitcast(F32)).then_inc(split_out[g % 2], 16)
                if g == 2:
                    store_y(tile, 0)
            store_y(tile, 1)

        for g in range(NG):
            sp.wait_ge(raw_out[g], 16 * (GATE_BLOCK + 1))
        sp.wait_ge(angles_done, 1)
        load_qkv(0, 0)
        for b in range(GATE_BLOCK, RAW_BLOCKS - 1):
            raw_block(b)
        load_qkv(1, 1)
        raw_block(RAW_BLOCKS - 1)
        for g in range(NG):
            sp.wait_ge(raw_out[g], 16 * (RAW_BLOCKS + 1))
        with sp.Fori(0, NT // 2 - 1) as i:
            for p in range(2):
                split_block(2 * i + p, True)
        split_block(NT - 2, True)
        split_block(NT - 1, False)

    @block.gpsimd
    def _(pool):
        chain = Chain(pool, pool_chain)

        pool.memset(power[:, :], -0.5).then_inc(consts_made, 1)
        for n in range(HALF):
            ins = pool.memset(inv_freq[:, n:n + 1], float(np.float32(THETA) ** np.float32(-n * 2.0 / HD)))
        ins.then_inc(consts_made, 1)
        chain.link(pool.memset(ident[:, :], 0.0))
        chain.link(pool.affine_select(out=ident[:, :], in_=ident[:, :], compare_op=ALU.not_equal, fill=1.0,
                                      base=0, pattern=[[-1, P]], channel_multiplier=1))
        pool.tensor_copy(ident_bf[:, :], ident[:, :]).then_inc(consts_made, 1)

        def split_half(b, p, h):
            at = slice(4 * h, 4 * h + 4)
            pool.wait_ge(w_loaded[h], 16 * (b + 1))
            pool.sem_inc(w_seen, 1)
            pool.tensor_copy(w_hi[:, p, at], w_raw[:, h]).then_inc(w_hi_done, 1)
            pool.wait_ge(w_hi_done, 2 * b + h + 1)
            pool.tensor_tensor(w_lo[:, p, at], w_raw[:, h], w_hi[:, p, at].bitcast(F32),
                               ALU.subtract).then_inc(w_split, 1)

        for n in range(NT):
            a = n % TPG
            pool.wait_ge(ms_done, n + 1)
            pool.tensor_tensor(rs[:, a:a + 1], ms[:, a:a + 1], power[:, 0:1], ALU.pow).then_inc(pow_done, 1)
            if n in (TPG, TPG + 2):
                split_half(0, 0, n // 2 - 2)
        split_half(1, 1, 0)
        split_half(1, 1, 1)

        chain.link(pool.memset(mask_even[:, :, :], 0.0))
        chain.link(pool.memset(mask_odd[:, :], 0.0))
        own = dict(compare_op=ALU.is_ge, fill=MASKED, base=0, pattern=[[-1, P]], channel_multiplier=1)
        before = dict(compare_op=ALU.is_gt, fill=MASKED, base=0, pattern=[[1, P]], channel_multiplier=-1)
        for n in range(2):
            chain.link(pool.affine_select(out=mask_even[:, n, 0:P], in_=mask_even[:, n, 0:P], **own))
        chain.link(pool.memset(mask_even[:, 0, P:], MASKED))
        chain.link(pool.affine_select(out=mask_even[:, 1, P:], in_=mask_even[:, 1, P:], **before))
        chain.link(pool.affine_select(out=mask_odd[:, 0:P], in_=mask_odd[:, 0:P], **before))
        pool.affine_select(out=mask_odd[:, P:], in_=mask_odd[:, P:], **own).then_inc(consts_made, 1)
        pool.memset(k_t[:, :, :, 1, :].bitcast(F32), 0.0).then_inc(consts_made, 1)
        pool.memset(v_s[:, 1].bitcast(F32), 0.0).then_inc(consts_made, 1)

        def split_w(b, p, free):
            pool.wait_ge(proj_done, free)
            for h in range(2):
                split_half(b, p, h)

        with pool.Fori(1, RAW_BLOCKS // 2) as i:
            for p in range(2):
                split_w(2 * i + p, p, NG * (2 * i + p - 1))

        def qk_power(n):
            pool.wait_ge(ms_done, NT + n + 1)
            pool.tensor_tensor(rs[:, :], ms[:, :], power[:, :], ALU.pow).then_inc(pow_done, 1)

        qk_power(0)
        with pool.Fori(RAW_BLOCKS // 2, (RAW_BLOCKS + SPLIT_BLOCKS) // 2) as i:
            for p in range(2):
                split_w(2 * i + p, p, NG * (2 * i + p - 1))
                qk_power(2 * i + p - RAW_BLOCKS + 1)

    @block.tensor
    def _(pe):
        from concourse.bass import ds
        mm = pe.matmul
        def project_part(p, g, part, parts):
            passes = [(w, h, k) for w, h in ((w_hi, ht_hi), (w_hi, ht_lo), (w_lo, ht_hi)) for k in range(KB)]
            per = len(passes) // parts
            for n in range(per * part, per * part + per):
                w, h, k = passes[n]
                ins = mm(bank[g], w[:, p, k, :], h[:, k, g * GRP:(g + 1) * GRP], start=n == 0,
                         stop=n == len(passes) - 1)
            if part == parts - 1:
                ins.then_inc(proj_done, 1)

        def tokens_out(n):
            pe.wait_ge(qkv_in, 16 * (n + 1))
            pe.wait_ge(k_ready, n)
            for j in range(6):
                ins = pe.transpose(X[:, j * P:(j + 1) * P], qkv_t[:, j, :], ident[:, :])
            ins.then_inc(tin_done, 1)

        def q_columns(n):
            pe.wait_ge(qk_out, n + 1)
            pe.wait_ge(qs_done, n + 1)
            for j in range(SWA_Q):
                ins = pe.transpose(X[:, j * P:(j + 1) * P], qk_split[:, j, :].bitcast(F32), ident[:, :])
            ins.then_inc(tq_done, 1)

        def k_columns(n):
            pe.wait_ge(q_ready, n + 1)
            for j in range(2 * SWA_KV):
                ins = pe.transpose(X[:, j * P:(j + 1) * P], qk_split[:, SWA_Q + j, :].bitcast(F32), ident[:, :])
            ins.then_inc(tk_done, 1)

        def scores(n, half, mask):
            pe.wait_ge(k_ready, n + 1)
            for j in (*range(GQ // 2, GQ), *range(GQ // 2)):
                if j == 0:
                    pe.wait_ge(y_read, 1 + 2 * n + half)
                out = Y[:, j * 2 * P:(j + 1) * 2 * P]
                mm(out, ident_bf[:, :], mask, start=True, stop=False)
                for s in range(2):
                    ins = mm(out, q_t[:, GQ * half + j, :], k_t[:, s, half, :, :].rearrange("p a b -> p (a b)"),
                             start=False, stop=s == 1)
            ins.then_inc(sc_done, 1)

        def probs_t(n, half):
            pe.wait_ge(p_done, 2 * n + half + 1)
            for s in range(2):
                for j in range(GQ):
                    at = (s * GQ + j) * P
                    ins = pe.transpose(Y[:, at:at + P], probs[:, j, s * P:(s + 1) * P], ident[:, :])
            ins.then_inc(pt_done, 1)

        def values(n, half):
            pe.wait_ge(v_done, n + 1)
            pe.wait_ge(p_split, 2 * n + half + 1)
            for s in range(2):
                for m, part in enumerate((p_hi, p_lo)):
                    ins = mm(Y[:, 0:GRP], v_s[:, s, half, :], part[:, s * GRP:(s + 1) * GRP],
                             start=s == 0 and m == 0, stop=s == 1 and m == 1)
            ins.then_inc(pv_done, 1)

        pe.wait_ge(consts_made, 3)
        for g in range(NG):
            for a in range(TPG):
                pe.wait_ge(x_scaled, TPG * g + a + 1)
                pe.wait_ge(ht_lo_done, TPG * g + a + 1)
                for k in range(KB):
                    ins = pe.transpose(x_t[a % 2][:, k * P:(k + 1) * P], x_in[:, a, k * P:(k + 1) * P], ident[:, :])
                ins.then_inc(xt_done, 1)
                if g == 2:
                    if a == 0:
                        pe.wait_ge(w_split, 2)
                    project_part(0, 0, a, TPG)
                if g == 3:
                    if a == 0:
                        pe.wait_ge(ht_lo_done, 2 + TPG * g)
                    project_part(0, 1 + a // 2, a % 2, 2)
        pe.wait_ge(ht_lo_done, 2 + NT)
        project_part(0, NG - 1, 0, 1)

        def raw_block(b, p):
            pe.wait_ge(w_split, 2 * (b + 1))
            for g in range(NG):
                pe.wait_ge(raw_done, NG * b + g + 1)
                project_part(p, g, 0, 1)

        raw_block(1, 1)
        with pe.Fori(1, RAW_BLOCKS // 2 - 1) as i:
            for p in range(2):
                raw_block(2 * i + p, p)
        pe.wait_ge(consts_made, 6)
        for p in range(2):
            b = RAW_BLOCKS - 2 + p
            pe.wait_ge(w_split, 2 * (b + 1))
            for g in range(NG):
                pe.wait_ge(raw_done, NG * b + g + 1)
                if (p, g) == (0, 1):
                    tokens_out(0)
                if (p, g) == (1, 0):
                    q_columns(0)
                if (p, g) == (1, 1):
                    k_columns(0)
                project_part(p, g, 0, 1)
        pe.wait_ge(raw_done, NG * (RAW_BLOCKS + 1))
        with pe.Fori(0, NT // 2) as i:
            for p in range(2):
                n = 2 * i + p
                b = n + RAW_BLOCKS
                if p:
                    mask = mask_odd[:, :]
                else:
                    mask = mask_even[:, :, :].rearrange("p a b -> p (a b)")[:, ds(((i + 7) // 8) * (2 * P), 2 * P)]
                pe.wait_ge(w_split, 2 * (b + 1))
                beside = {0: [tokens_out], 1: [scores], 6: [probs_t], 8: [values], 10: [scores], 12: [q_columns],
                          14: [probs_t], 15: [k_columns], 16: [values]}
                for h in range(4 * NG + 1):
                    for stage in beside.get(h, ()):
                        if stage is scores:
                            scores(n, h // 10, mask)
                        elif stage in (probs_t, values):
                            stage(n, h // 10)
                        else:
                            stage(n + 1)
                    if h < 4 * NG:
                        g, part = h // 4, h % 4
                        if part == 0:
                            pe.wait_ge(split_done, NG * n + g + 1)
                        project_part(p, g, part, 4)

    @block.scalar
    def _(act):
        from concourse.bass import ds
        act.sem_inc(raw_done, NG)
        act.sem_inc(split_done, NG)
        act.sem_inc(ht_lo_done, 2)
        act.sem_inc(y_gated, 1)
        act.sem_inc(y_read, 1)
        act.sem_inc(y_out, 16)
        for s in (*raw_out, *split_out):
            act.sem_inc(s, 16)

        def squares(g, a, first=False):
            act.wait_ge(x_loaded[a], 16 * (g + 1))
            if not first:
                act.wait_ge(ssq_done, TPG * g + a)
            act.activation(stage_hi[:, :, :].rearrange("p a b -> p (a b)"), x_in[:, a, :], ACT.Square,
                           accum_out=ssq[:, a:a + 1]).then_inc(ssq_done, 1)

        def norm_turn(g, more):
            for a in range(TPG):
                if more or a + 2 < TPG:
                    squares(g + (a + 2) // TPG, (a + 2) % TPG)
                act.wait_ge(xt_done, TPG * g + a + 1)
                act.activation(ht_hi[:, :, ds(g * GRP + a * P, P)], x_t[a % 2][:, :].rearrange("p (k t) -> p k t", k=KB),
                               ACT.Copy).then_inc(ht_hi_done, 1)

        squares(0, 0, True)
        squares(0, 1)
        with act.Fori(0, NG - 1) as g:
            norm_turn(g, True)
        norm_turn(NG - 1, False)

        def tile_in(n):
            act.wait_ge(v_done, n)
            act.wait_ge(tin_done, n + 1)
            act.activation(qkv.rearrange("p h d -> p (h d)"), X[:, 0:6 * P], ACT.Copy).then_inc(qk_out, 1)

        def v_high(n, p):
            act.wait_ge(pv_done, 2 * n)
            act.activation(v_s[:, p, :, 0:HD], v_raw, ACT.Copy).then_inc(v_hi_done, 1)

        def high_parts(n):
            act.wait_ge(rot_done, n + 1)
            act.wait_ge(tk_done, n)
            act.activation(qk_split[:, 0:QK, 0:HALF], rot1, ACT.Copy).then_inc(qs_hi_done, 1)
            act.activation(qk_split[:, 0:QK, HALF:HD], qk[:, :, HALF:HD], ACT.Copy).then_inc(qs_hi_done, 1)

        def swapped_k(n):
            act.wait_ge(qs_lo_done, n + 1)
            act.wait_ge(qs_hi_done, 2 * (n + 1))
            act.activation(qk_split[:, QK:, 0:HD], qk_split[:, SWA_Q:QK, HD:P].bitcast(F32), ACT.Copy)
            act.activation(qk_split[:, QK:, HD:P], qk_split[:, SWA_Q:QK, 0:HD].bitcast(F32),
                           ACT.Copy).then_inc(qs_done, 1)

        def q_out(n):
            act.wait_ge(tq_done, n + 1)
            act.wait_ge(sc_done, 2 * n)
            act.activation(q_t[:, :, :].rearrange("p a b -> p (a b)"), X[:, :], ACT.Copy).then_inc(q_ready, 1)

        def k_out(n, p):
            act.wait_ge(tk_done, n + 1)
            act.activation(k_t[:, :, :, p, :].rearrange("p a b c -> p (a b) c"),
                           X[:, 0:GRP].rearrange("p (a b) -> p a b", a=4), ACT.Copy).then_inc(k_ready, 1)

        def softmax(n, half):
            act.wait_ge(top_done, 2 * n + half + 1)
            for j in range(GQ):
                act.activation(probs[:, j, :], Y[:, j * 2 * P:(j + 1) * 2 * P], ACT.Exp, bias=neg_top[:, j:j + 1],
                               scale=SCALE, accum_out=den[:, j:j + 1])
            act.activation(sink_e[:, :], sink_e[:, :], ACT.Exp).then_inc(exp_done, 1)

        def p_high(n, half):
            act.wait_ge(pt_done, 2 * n + half + 1)
            act.activation(p_hi[:, :], Y[:, :], ACT.Copy).then_inc(p_hi_done, 1)

        def low_values(n, half):
            act.wait_ge(pv_done, 2 * n + half + 1)
            act.activation(y_sum, Y[HD:P, 0:GRP].rearrange("p (a b) -> p a b", a=GQ), ACT.Copy).then_inc(yv_done, 1)

        def raw_group(b, g):
            act.wait_ge(proj_done, NG * b + g + 1)
            act.wait_ge(raw_out[g], 16 + 16 * b)
            act.activation(stage_raw[:, g, :], bank[g], ACT.Copy).then_inc(raw_done, 1)

        def gate_group(b, g):
            act.wait_ge(proj_done, NG * b + g + 1)
            act.wait_ge(raw_out[g], 16 + 16 * b)
            act.activation(stage_raw[:, g, :], bank[g], ACT.Sigmoid).then_inc(sigmoid_done, 1)

        with act.Fori(0, GATE_BLOCK // 2) as i:
            for p in range(2):
                for g in range(NG):
                    raw_group(2 * i + p, g)
        act.wait_ge(angles_done, 1)
        act.activation(sin, sin, ACT.Sin).then_inc(rope_done, 1)
        act.activation(cos, cos, ACT.Sin).then_inc(rope_done, 1)
        for p in range(2):
            for g in range(NG):
                gate_group(GATE_BLOCK + p, g)
        b = RAW_BLOCKS - 2
        gate_group(b, 0)
        tile_in(0)
        gate_group(b, 1)
        high_parts(0)
        gate_group(b, 2)
        swapped_k(0)
        gate_group(b, 3)
        q_out(0)
        gate_group(b + 1, 0)
        k_out(0, 0)
        v_high(0, 0)
        for g in range(1, NG):
            gate_group(b + 1, g)
        for g in range(NG):
            act.wait_ge(raw_out[g], 16 * (RAW_BLOCKS + 1))

        with act.Fori(0, NT // 2) as i:
            for p in range(2):
                n = 2 * i + p

                def block_high(g):
                    act.wait_ge(proj_done, NG * (n + RAW_BLOCKS) + g + 1)
                    act.wait_ge(split_out[g % 2], 16 + 32 * (2 * n + g // 2))
                    act.activation(stage_hi[:, g % 2, :], bank[g], ACT.Copy).then_inc(hi_done, 1)

                tile_in(n + 1)
                softmax(n, 0)
                block_high(0)
                p_high(n, 0)
                block_high(1)
                high_parts(n + 1)
                low_values(n, 0)
                swapped_k(n + 1)
                softmax(n, 1)
                block_high(2)
                q_out(n + 1)
                p_high(n, 1)
                k_out(n + 1, 1 - p)
                low_values(n, 1)
                block_high(3)
                v_high(n + 1, 1 - p)

    @block.vector
    def _(dve):
        from concourse.bass import ds
        chain = Chain(dve, dve_chain)

        def mean(g, a):
            dve.wait_ge(ssq_done, TPG * g + a + 1)
            dve.tensor_scalar(ms[:, a:a + 1], ssq[:, a:a + 1], 1.0 / D_MODEL, EPS, ALU.mult, ALU.add).then_inc(ms_done, 1)

        def low(g, a):
            dve.wait_ge(ht_hi_done, TPG * g + a + 1)
            at = ds(g * GRP + a * P, P)
            dve.tensor_tensor(ht_lo[:, :, at], x_t[a % 2][:, :].rearrange("p (k t) -> p k t", k=KB),
                              ht_hi[:, :, at].bitcast(F32), ALU.subtract).then_inc(ht_lo_done, 1)

        def newton_first(g, a):
            y = rs[:, a:a + 1]
            dve.wait_ge(pow_done, TPG * g + a + 1)
            chain.mark(dve.scalar_tensor_tensor(rtmp[:, a:a + 1], ms[:, a:a + 1], y, y, ALU.mult, ALU.mult))

        def newton_second(a):
            chain.wait()
            chain.mark(dve.tensor_scalar(rtmp[:, a:a + 1], rtmp[:, a:a + 1], -0.5, 1.5, ALU.mult, ALU.add))

        def scaled(a):
            y = rs[:, a:a + 1]
            chain.wait()
            chain.link(dve.tensor_tensor(y, y, rtmp[:, a:a + 1], ALU.mult))
            dve.scalar_tensor_tensor(x_in[:, a, :], x_in[:, a, :], y, gain, ALU.mult, ALU.mult).then_inc(x_scaled, 1)

        def norm_turn(g, more):
            for a in range(TPG):
                norm, means = more or a + 2 < TPG, more or a + 3 < TPG
                if norm:
                    newton_first(g + (a + 2) // TPG, (a + 2) % TPG)
                low(g, a)
                if norm:
                    newton_second((a + 2) % TPG)
                if means:
                    mean(g + (a + 3) // TPG, (a + 3) % TPG)
                if norm:
                    scaled((a + 2) % TPG)

        for a in range(2):
            mean(0, a)
        dve.wait_ge(gain_in, 16)
        for a in range(2):
            newton_first(0, a)
            newton_second(a)
            scaled(a)
            if a == 0:
                mean(0, 2)
        with dve.Fori(0, NG - 1) as g:
            chain.enter(g, 3 * TPG)
            norm_turn(g, True)
        chain.leave(NG - 1)
        norm_turn(NG - 1, False)

        ang, turns, tmp = rope_tmp
        flat = lambda v: v.rearrange("p a b -> p (a b)")
        dve.wait_ge(pos_in, 16)
        dve.wait_ge(consts_made, 2)
        chain.link(dve.tensor_copy(pos[:, :], pos_i[:, :]))
        dve.wait_ge(xt_done, NT)
        dve.wait_ge(x_scaled, NT)
        chain.link(dve.tensor_tensor(ang, spread(pos[:, :], HALF, 2), spread(inv_freq[:, :], NT, 1), ALU.mult))
        for whole in (4096.0, 1.0):
            chain.link(dve.tensor_scalar(flat(turns), flat(ang), 1.0 / (2 * np.pi * whole), ROUND, ALU.mult, ALU.add))
            chain.link(dve.tensor_scalar(flat(turns), flat(turns), -ROUND, None, ALU.add))
            for part in TWO_PI_PARTS:
                chain.link(dve.scalar_tensor_tensor(flat(ang), flat(turns), -part * whole, flat(ang), ALU.mult, ALU.add))
        chain.link(dve.tensor_scalar(flat(sin), flat(ang), PI, -PI, ALU.min, ALU.max))
        chain.link(dve.tensor_scalar(flat(cos), flat(ang), np.pi / 2, None, ALU.add))
        chain.link(dve.tensor_scalar(flat(tmp), flat(cos), PI, -2 * np.pi, ALU.is_gt, ALU.mult))
        chain.link(dve.tensor_tensor(flat(cos), flat(cos), flat(tmp), ALU.add))
        dve.tensor_scalar(flat(cos), flat(cos), PI, -PI, ALU.min, ALU.max).then_inc(angles_done, 1)

        def gate_groups(m):
            for g in range(NG):
                dve.wait_ge(sigmoid_done, NG * m + g + 1)
                dve.tensor_tensor(stage_raw[:, g, :], bank[g], stage_raw[:, g, :], ALU.mult).then_inc(raw_done, 1)

        def v_low(n, p):
            dve.wait_ge(v_hi_done, n + 1)
            dve.tensor_tensor(v_s[:, p, :, HD:P], v_raw, v_s[:, p, :, 0:HD].bitcast(F32),
                              ALU.subtract).then_inc(v_done, 1)

        def head_squares(n):
            dve.wait_ge(qk_out, n + 1)
            rot_all = rot.rearrange("p a (h d) -> p (a h) d", d=HD)
            chain.link(dve.tensor_tensor(rot_all, qk, qk, ALU.mult))
            chain.link(dve.tensor_reduce(ssq[:, :], rot_all, AX.X, ALU.add))
            dve.tensor_scalar(ms[:, :], ssq[:, :], 1.0 / HD, EPS, ALU.mult, ALU.add).then_inc(ms_done, 1)

        def norm(n):
            dve.wait_ge(pow_done, NT + n + 1)
            newton_rsqrt(dve, chain, rs[:, :], ms[:, :], rtmp[:, :])
            chain.link(dve.tensor_tensor(qk, qk, spread(rs[:, :], HD, 2), ALU.mult))
            dve.tensor_tensor(qk[:, 0:SWA_Q, :], qk[:, 0:SWA_Q, :], spread(qk_gain[:, 0, :], SWA_Q, 1), ALU.mult)
            chain.link(dve.tensor_tensor(qk[:, SWA_Q:, :], qk[:, SWA_Q:, :], spread(qk_gain[:, 1, :], SWA_KV, 1),
                                         ALU.mult))

        def rotate(tile):
            c_t = spread(cos[:, tile, :], QK, 1)
            s_t = spread(sin[:, tile, :], QK, 1)
            x1, x2 = qk[:, :, 0:HALF], qk[:, :, HALF:HD]
            dve.tensor_tensor(rot1, x1, c_t, ALU.mult)
            chain.link(dve.tensor_tensor(rot2, x2, s_t, ALU.mult))
            chain.link(dve.tensor_tensor(rot1, rot1, rot2, ALU.subtract))
            dve.tensor_tensor(x2, x2, c_t, ALU.mult)
            chain.link(dve.tensor_tensor(rot2, x1, s_t, ALU.mult))
            dve.tensor_tensor(x2, x2, rot2, ALU.add).then_inc(rot_done, 1)

        def low_parts(n):
            dve.wait_ge(qs_hi_done, 2 * (n + 1))
            dve.wait_ge(rot_done, n + 1)
            dve.tensor_tensor(qk_split[:, 0:QK, HD:HD + HALF], rot1, qk_split[:, 0:QK, 0:HALF].bitcast(F32), ALU.subtract)
            dve.tensor_tensor(qk_split[:, 0:QK, HD + HALF:P], qk[:, :, HALF:HD],
                              qk_split[:, 0:QK, HALF:HD].bitcast(F32), ALU.subtract).then_inc(qs_lo_done, 1)

        def top_score(n, half):
            dve.wait_ge(sc_done, 2 * n + half + 1)
            sinks = sink[:, GQ * half:GQ * half + GQ]
            chain.link(dve.tensor_reduce(top[:, :], Y[:, :].rearrange("p (a b) -> p a b", a=GQ), AX.X, ALU.max))
            chain.link(dve.scalar_tensor_tensor(top[:, :], top[:, :], SCALE, sinks, ALU.mult, ALU.max))
            dve.tensor_scalar(neg_top[:, :], top[:, :], -1.0, None, ALU.mult)
            dve.tensor_tensor(sink_e[:, :], sinks, top[:, :], ALU.subtract).then_inc(top_done, 1)

        def normalise(n, half):
            dve.wait_ge(exp_done, 2 * n + half + 1)
            chain.link(dve.tensor_tensor(den[:, :], den[:, :], sink_e[:, :], ALU.add))
            chain.link(dve.reciprocal(den[:, :], den[:, :]))
            dve.tensor_tensor(probs, probs, spread(den[:, :], 2 * P, 2), ALU.mult).then_inc(p_done, 1)

        def p_low(n, half):
            dve.wait_ge(p_hi_done, 2 * n + half + 1)
            dve.tensor_tensor(p_lo[:, :], Y[:, :], p_hi[:, :].bitcast(F32), ALU.subtract).then_inc(p_split, 1)

        def weighted(n, half):
            dve.wait_ge(yv_done, 2 * n + half + 1)
            dve.tensor_tensor(y_sum, y_sum, Y[0:HD, 0:GRP].rearrange("p (a b) -> p a b", a=GQ),
                              ALU.add).then_inc(y_read, 1)
            dve.wait_ge(y_read, 1 + 2 * n + half + 1)
            dve.wait_ge(gate_in, 16 * (n + 1))
            gates = gate_t[:, GQ * half:GQ * half + GQ, :]
            dve.tensor_tensor(gates, y_sum, gates, ALU.mult).then_inc(y_gated, 1)

        gate_groups(0)
        gate_groups(1)
        dve.wait_ge(rope_done, 2)
        dve.wait_ge(consts_in, 48)
        head_squares(0)
        norm(0)
        rotate(0)
        low_parts(0)
        gate_groups(2)
        v_low(0, 0)
        gate_groups(3)
        with dve.Fori(0, NT // 2) as i:
            chain.enter(i, 2 * SWA_TURN)
            for p in range(2):
                n = 2 * i + p
                nxt = (n + 1) % NT

                def block_low(g):
                    dve.wait_ge(hi_done, NG * n + g + 1)
                    dve.tensor_tensor(stage_lo[:, g % 2, :], bank[g], stage_hi[:, g % 2, :].bitcast(F32),
                                      ALU.subtract).then_inc(split_done, 1)

                top_score(n, 0)
                head_squares(n + 1)
                normalise(n, 0)
                block_low(0)
                norm(n + 1)
                p_low(n, 0)
                rotate(nxt)
                block_low(1)
                weighted(n, 0)
                low_parts(n + 1)
                top_score(n, 1)
                normalise(n, 1)
                block_low(2)
                p_low(n, 1)
                weighted(n, 1)
                block_low(3)
                v_low(n + 1, 1 - p)
        chain.leave(NT // 2)


SWA_TURN = 19


PAIRS = SEQ // (2 * P)
TURNS = SB_H // 2
Z_BANKS, WT_SLOTS = 4, 3
SHORT = 2
W_SLOTS = 4


class Sticks:

    UNITS = 2 * PAIRS
    V_TURN = 2 * NT // 4

    def __init__(self):
        self.pieces, self.chunk0 = {}, {}
        z = k = 0
        for n in range(self.UNITS):
            j = self.unit(n)[1]
            self.pieces[n] = [(z + m, *cut) for m, cut in enumerate(self.cuts(j))]
            self.chunk0[n] = k
            z, k = z + len(self.pieces[n]), k + j + 1
        self.Z_TURN, self.K_TURN, self.T_TURN = z, k, k + self.V_TURN
        self.pieces[self.UNITS] = [(z + first, *cut) for first, *cut in self.pieces[0]]
        assert z % Z_BANKS == 0 and k % WT_SLOTS == 0 and self.T_TURN % 2 == 0

    @staticmethod
    def unit(n):
        return (0, PAIRS - 1 - n) if n < PAIRS else (1, n - PAIRS) if n < 2 * PAIRS else (0, PAIRS - 1)

    @staticmethod
    def cuts(j):
        ends = [P * (2 * j + 1), P * (2 * j + 2)]
        return [(s, k0, min(GRP, ends[s] - k0)) for k0 in range(ends[1] // GRP * GRP, -1, -GRP)
                for s in range(2) if k0 < ends[s]]

    def order(self, more):
        out, x = [], 0
        for n in range(self.UNITS):
            slot, j = self.unit(n)
            pieces = self.pieces[n + 1] if more or n + 1 < self.UNITS else []
            for c in range(j + 1):
                out += [("piece", n + 1, q) for m, q in enumerate(pieces) if m * (j + 1) // len(pieces) == c]
                out.append(("chunk", self.chunk0[n] + c, n, j - c, x))
                x += 1
                if j == PAIRS - 3 and 1 <= c <= NT // 4 and (slot == 0 or more):
                    out.append(("v", 1 - slot, c - 1, x))
                    x += 1
        return out

    def needed(self, n, m):
        return max(z for z, _, k0, _ in self.pieces[n] if k0 == 2 * m * P // GRP * GRP)

    def last_chunk(self, n):
        return self.chunk0[n] + self.unit(n)[1]


def sticks(nc, c, t, stores, wo):
    from concourse.bass import ds
    o = Sticks()
    sb = lambda n, s, d=F32: c.enter_context(nc.sbuf_tensor(n, s, d))
    sem = lambda n: c.enter_context(nc.semaphore(n))
    ident, ident_bf = sb("identb", [P, P]), sb("identb_bf", [P, P], BF16)
    twice = sb("twice", [P, P], F32R)
    mask = sb("mask", [P, P], BF16)
    q_s = sb("q_s", [P, 2, SEQ], F32R)
    k_s = sb("k_s", [P, 2, 2, SEQ], F32R)
    v_s = sb("vb_s", [P, 2, NT, P])
    take = sb("take", [P, 4, SEQ])
    twice_f = take[:, 3, 0:P]
    left = sb("left", [P, 4, SEQ])
    v_t = sb("v_t", [P, SEQ], F32R)
    wt = sb("wt", [P, WT_SLOTS, 4 * P])
    gate_hi, gate_lo, gate = sb("gate_hi", [P, SEQ]), sb("gate_lo", [P, SEQ]), sb("gate", [P, SEQ])
    y, y_out = wo.yb, wo.yb_out
    Z = [c.enter_context(nc.psum_tensor(f"Z{s}", [P, GRP], F32)) for s in range(Z_BANKS)]
    T = [c.enter_context(nc.psum_tensor(f"T{s}", [P, 4 * P], F32)) for s in range(2)]
    O = [c.enter_context(nc.psum_tensor(f"O{s}", [P, 4 * P], F32)) for s in range(2)]
    consts, chain_sem = sem("b_consts"), sem("b_chain")
    late_in = sem("late_in")
    head_in = [sem(f"head_in{p}") for p in range(2)]
    v_in, gate_in, gate_sum, gate_sig, gate_done = (sem(n) for n in (
        "v_in", "b_gate_in", "gate_sum", "gate_sig", "gate_done"))
    z_done, z_read, scanned, w_done = sem("z_done"), sem("z_read"), sem("scanned"), sem("w_done")
    t_done, t_read, pv_done, gated = sem("t_done"), sem("t_read"), sem("b_pv_done"), sem("gated")
    q_rest_in = sem("q_rest_in")
    Z0, PV0, O0 = Z_BANKS, WT_SLOTS, 2
    T0 = NT // 4

    HB = SB_H * HD
    HEAD_LOADS = 16 * 6
    FIRST_K = 16 * 4
    LATE, REST = slice(SEQ - GRP, SEQ), slice(0, SEQ - GRP)

    block = c.enter_context(nc.Block())

    @block.sync
    def _(sp):
        def rows(name, kind, head):
            return t[name][ds(kind * HB + head * HD, HD), :]

        def load_q(head, p, done, at=slice(0, SEQ)):
            for half, name in enumerate(("hi", "lo")):
                to = slice(half * HD, half * HD + HD)
                sp.dma_start(q_s[to, p, at].bitcast(F32), rows(name, 0, head)[:, at]).then_inc(done, 16)

        def load_k(head, p, done, at=slice(0, SEQ)):
            for half, names in enumerate((("hi", "lo"), ("lo", "hi"))):
                to = slice(half * HD, half * HD + HD)
                for m, name in enumerate(names):
                    sp.dma_start(k_s[to, p, m, at].bitcast(F32), rows(name, 1, head)[:, at]).then_inc(done, 16)

        def load_v(head):
            for half, name in enumerate(("hi", "lo")):
                sp.dma_start(v_t[half * HD:half * HD + HD, :].bitcast(F32), rows(name, 2, head)).then_inc(v_in, 16)

        def load_gate(pair):
            sp.dma_start(gate_hi[:, :], t["hi"][ds(3 * HB + pair * P, P), :]).then_inc(gate_in, 16)
            sp.dma_start(gate_lo[:, :], t["lo"][ds(3 * HB + pair * P, P), :]).then_inc(gate_in, 16)

        def turn(i, more):
            if more:
                sp.wait_ge(gate_done, i + 1)
                load_gate(i + 1)
            v_last = [max(step[3] for step in o.order(True) if step[0] == "v" and step[1] == p) for p in range(2)]
            for p in range(2):
                last = o.pieces[PAIRS * (p + 1) - 1][-1][0]
                if more:
                    sp.wait_ge(t_done, T0 + o.T_TURN * i + v_last[1 - p] + 1)
                    load_v(2 * i + 2 + p)
                    sp.wait_ge(z_done, o.Z_TURN * i + last + 1)
                    load_q(2 * i + 2 + p, p, head_in[p])
                    load_k(2 * i + 2 + p, p, head_in[p])
                sp.wait_ge(gated, O0 + o.UNITS * i + PAIRS * (p + 1))
                sp.dma_start(t["y"][ds(SWA_Q * HD + i * P + p * HD, HD), :],
                             y[p * HD:p * HD + HD, :]).then_inc(y_out[p], 16)

        load_q(0, 0, late_in, LATE)
        load_k(0, 0, late_in, LATE)
        sp.wait_ge(stores.y_out, 16 + 16 * 2 * NT)
        for s in range(2):
            sp.wait_ge(stores.split_out[s], 16 + 16 * 2 * 2 * NT)
        load_k(0, 0, head_in[0], REST)
        load_v(0)
        load_q(0, 0, q_rest_in, REST)
        load_gate(0)
        load_q(1, 1, head_in[1])
        load_k(1, 1, head_in[1])
        sp.wait_ge(t_done, T0)
        load_v(1)
        with sp.Fori(0, TURNS - 1) as i:
            turn(i, True)
        for k in range(W_SLOTS):
            sp.dma_start(wo.raw[:, k, :], wo.view[:, k, :]).then_inc(wo.loaded[k], 16)
        for s in range(TPG):
            sp.dma_start(wo.ya[:, s], wo.ya_view[:, :, s * P:(s + 1) * P]).then_inc(wo.ya_in[s], 16)
        turn(TURNS - 1, False)

    @block.gpsimd
    def _(pool):
        chain = Chain(pool, chain_sem)
        diagonal = lambda m, base: chain.link(pool.affine_select(
            out=m, in_=m, compare_op=ALU.not_equal, fill=1.0, base=base, pattern=[[-1, P]], channel_multiplier=1))
        chain.link(pool.memset(ident[:, :], 0.0))
        diagonal(ident[:, :], 0)
        chain.link(pool.tensor_copy(ident_bf[:, :], ident[:, :]))
        chain.link(pool.memset(mask[:, :], 0.0))
        chain.link(pool.memset(twice_f, 0.0))
        for base in (0, HD, -HD):
            diagonal(twice_f, base)
        chain.link(pool.tensor_copy(twice[:, :], twice_f))
        pool.affine_select(out=mask[:, :], in_=mask[:, :], compare_op=ALU.is_gt, fill=MASKED, base=0,
                           pattern=[[-1, P]], channel_multiplier=1).then_inc(consts, 1)

    @block.tensor
    def _(pe):
        mm = pe.matmul

        def scores(i, n, piece):
            z, s, k0, keys = piece
            p, j = o.unit(n)
            a = 2 * j + s
            out = Z[z % Z_BANKS]
            pe.wait_ge(z_read, Z0 + o.Z_TURN * i + z - Z_BANKS + 1)
            last = k0 + keys == P * (a + 1)
            for part in range(2):
                ins = mm(out[:, 0:keys], q_s[:, p, a * P:(a + 1) * P],
                         k_s[:, p, part, k0:k0 + keys], start=part == 0, stop=part == 1 and not last)
            if last:
                ins = mm(out[:, keys - P:keys], ident_bf[:, :], mask[:, :], start=False, stop=True)
            ins.then_inc(z_done, 1)

        def columns_v(i, m, x):
            if x >= 2 - T0:
                pe.wait_ge(t_read, T0 + o.T_TURN * i + x - 1)
            for b in range(4):
                ins = mm(T[x % 2][:, b * P:(b + 1) * P], v_t[:, (4 * m + b) * P:(4 * m + b + 1) * P],
                         twice[:, :], start=True, stop=True)
            ins.then_inc(t_done, 1)

        def transpose_w(i, n, m, x):
            pe.wait_ge(t_read, T0 + o.T_TURN * i + x - 1)
            blocks = [(2 * m, 0), (2 * m, 1), (2 * m + 1, 0), (2 * m + 1, 1)]
            if m == o.unit(n)[1]:
                blocks.remove((2 * m + 1, 0))
            pe.wait_ge(w_done, o.Z_TURN * i + o.needed(n, m) + 1)
            for b, (kb, s) in enumerate(blocks):
                ins = pe.transpose(T[x % 2][:, b * P:(b + 1) * P], take[:, (2 * n + s) % 4, kb * P:(kb + 1) * P],
                                   ident[:, :])
            ins.then_inc(t_done, 1)

        def values(i, k, n, m, x):
            p, j = o.unit(n)
            pe.wait_ge(t_read, T0 + o.T_TURN * i + x + 1)
            if m == j:
                pe.wait_ge(gated, O0 + o.UNITS * i + n - 1)
            for b in range(2):
                at, first = (2 * P, P) if m == j and b else (b * 2 * P, 0)
                ins = mm(O[n % 2][:, first:2 * P], v_s[:, p, 2 * m + b, :], wt[:, k % WT_SLOTS, at:at + 2 * P - first],
                         start=m == j and b == 0, stop=m == 0 and b == 1)
            ins.then_inc(pv_done, 1)

        def turn(i, more):
            waiting = []
            for kind, *step in o.order(more):
                if kind == "piece":
                    if step[0] == PAIRS and step[1] == o.pieces[PAIRS][0]:
                        pe.wait_ge(head_in[1], HEAD_LOADS * (i + 1))
                    if step[0] == 2 and step[1] == o.pieces[2][0]:
                        pe.wait_ge(q_rest_in, 32)
                    if step[0] == o.UNITS and step[1] == o.pieces[o.UNITS][0]:
                        pe.wait_ge(head_in[0], FIRST_K + HEAD_LOADS * (i + 1))
                    scores(i, *step)
                elif kind == "v":
                    slot, m, x = step
                    if m == 0:
                        pe.wait_ge(v_in, 32 * (2 * i + 3 - slot))
                    columns_v(i, m, x)
                else:
                    k, n, m, x = step
                    transpose_w(i, n, m, x)
                    waiting.append(step)
                    if len(waiting) == WT_SLOTS:
                        values(i, *waiting.pop(0))
            for chunk in waiting:
                values(i, *chunk)

        pe.wait_ge(consts, 1)
        pe.wait_ge(late_in, HEAD_LOADS)
        for piece in o.pieces[0]:
            if piece[2] < LATE.start:
                pe.wait_ge(head_in[0], FIRST_K)
            scores(0, 0, piece)
        pe.wait_ge(v_in, 32)
        for m in range(T0):
            columns_v(0, m, m - T0)
        with pe.Fori(0, TURNS - 1) as i:
            turn(i, True)
        turn(TURNS - 1, False)

    @block.scalar
    def _(act):
        act.sem_inc(z_read, Z0)
        act.sem_inc(pv_done, PV0)
        act.sem_inc(gated, O0)
        for s in range(2):
            act.sem_inc(y_out[s], 16)

        def sigmoids(i, n, piece, x_last=None):
            z, s, k0, keys = piece
            tile = (2 * n + s) % 4
            if n and piece == o.pieces[n][0]:
                before = x_last[n - 2] + 1 if n > 1 else 0
                act.wait_ge(t_done, T0 + o.T_TURN * i + before)
            act.wait_ge(z_done, o.Z_TURN * i + z + 1)
            bank = Z[z % Z_BANKS][:, 0:keys]
            act.activation(left[:, tile, k0:k0 + keys], bank, ACT.Sigmoid, scale=-SCALE)
            act.activation(take[:, tile, k0:k0 + keys], bank, ACT.Sigmoid, scale=SCALE).then_inc(z_read, 1)

        def copy_v(i, p, m, x):
            act.wait_ge(t_done, T0 + o.T_TURN * i + x + 1)
            act.activation(v_s[:, p, 4 * m:4 * m + 4, :].rearrange("p a b -> p (a b)"), T[x % 2][:, :],
                           ACT.Copy).then_inc(t_read, 1)

        def copy_w(i, k, n, m, x):
            w = 3 * P if m == o.unit(n)[1] else 4 * P
            act.wait_ge(t_done, T0 + o.T_TURN * i + x + 1)
            act.wait_ge(pv_done, PV0 + o.K_TURN * i + k - WT_SLOTS + 1)
            act.activation(wt[:, k % WT_SLOTS, 0:w], T[x % 2][:, 0:w], ACT.Copy).then_inc(t_read, 1)

        def turn(i, more):
            x_last = {}
            for kind, *step in o.order(more):
                if kind == "piece":
                    sigmoids(i, *step, x_last)
                elif kind == "v":
                    if step[1] == 0:
                        act.wait_ge(pv_done, PV0 + o.K_TURN * i + (0 if step[0] else o.chunk0[PAIRS]))
                    copy_v(i, *step)
                else:
                    copy_w(i, *step)
                    x_last[step[1]] = step[3]
                    if step[0] == GATE_STEPS[1]:
                        act.wait_ge(gate_sum, i + 1)
                        act.activation(gate_lo[:, :], gate[:, :], ACT.Sigmoid).then_inc(gate_sig, 1)

        for piece in o.pieces[0]:
            sigmoids(0, 0, piece)
        for m in range(T0):
            copy_v(0, 0, m, m - T0)
        with act.Fori(0, TURNS - 1) as i:
            turn(i, True)
        turn(TURNS - 1, False)

    @block.vector
    def _(dve):
        def products(i, n, piece):
            z, s, k0, keys = piece
            tile = (2 * n + s) % 4
            at = left[:, tile, k0:k0 + keys][:, ::-1]
            first = k0 + keys == P * (2 * o.unit(n)[1] + s + 1)
            dve.wait_ge(z_read, Z0 + o.Z_TURN * i + z + 1)
            if not first:
                before = max(b for b, s1, _, _ in o.pieces[n] if s1 == s and b < z)
                dve.wait_ge(scanned, o.Z_TURN * i + before + 1)
            dve.tensor_tensor_scan(at, at, at, 1.0 if first else left[:, tile, k0 + keys:k0 + keys + 1],
                                   ALU.mult, ALU.min).then_inc(scanned, 1)

        def weights(i, n, piece):
            z, s, k0, keys = piece
            tile = (2 * n + s) % 4
            if k0 + keys == P * (2 * o.unit(n)[1] + s + 1):
                keys -= 1
            dve.wait_ge(scanned, o.Z_TURN * i + z + 1)
            at = take[:, tile, k0:k0 + keys]
            dve.tensor_tensor(at, at, left[:, tile, k0 + 1:k0 + keys + 1], ALU.mult).then_inc(w_done, 1)

        def gate_sums(i, n):
            p, j = o.unit(n)
            at, cols = slice(p * HD, p * HD + HD), slice(j * 2 * P, (j + 1) * 2 * P)
            dve.wait_ge(pv_done, PV0 + o.K_TURN * i + o.last_chunk(n) + 1)
            if n % PAIRS == 0:
                dve.wait_ge(y_out[p], 16 * (i + 1))
            dve.tensor_tensor(y[at, cols], O[n % 2][at, 0:2 * P], gate[at, cols], ALU.mult).then_inc(gated, 1)

        def turn(i, more):
            multiplied = (0, o.pieces[0][-1])
            for kind, *step in o.order(more):
                if kind == "piece":
                    products(i, *step)
                    if multiplied:
                        weights(i, *multiplied)
                    multiplied = step
                    n, piece = step
                    if o.unit(n)[1] < SHORT and piece == o.pieces[n][-1]:
                        weights(i, *multiplied)
                        multiplied = None
                elif kind == "chunk":
                    if not more and multiplied and step[0] == o.chunk0[o.UNITS - 1]:
                        weights(i, *multiplied)
                    k, n, m, x = step
                    if k == GATE_STEPS[0]:
                        dve.wait_ge(gate_in, 32 * (i + 1))
                        dve.tensor_tensor(gate[:, :], gate_hi[:, :], gate_lo[:, :], ALU.add).then_inc(gate_sum, 1)
                    if k == GATE_STEPS[2]:
                        dve.wait_ge(gate_sig, i + 1)
                        dve.tensor_tensor(gate[:, :], gate[:, :], gate_lo[:, :], ALU.mult).then_inc(gate_done, 1)
                        dve.wait_ge(gate_done, i + 1)
                    for n in range(o.UNITS):
                        if k == o.last_chunk(n) + WT_SLOTS:
                            gate_sums(i, n)
            for n in range(o.UNITS):
                if o.last_chunk(n) + WT_SLOTS >= o.K_TURN:
                    gate_sums(i, n)

        for piece in o.pieces[0]:
            products(0, 0, piece)
            if piece != o.pieces[0][0]:
                weights(0, 0, o.pieces[0][piece[0] - 1])
        with dve.Fori(0, TURNS - 1) as i:
            turn(i, True)
        turn(TURNS - 1, False)


GATE_STEPS = (3, 5, 8)


class Stores:

    def __init__(self, nc, c):
        self.split_out = [c.enter_context(nc.semaphore(f"split_out{s}")) for s in range(2)]
        self.y_out = c.enter_context(nc.semaphore("y_out"))


class MixInputs:

    def __init__(self, nc, c, t):
        self.raw = c.enter_context(nc.sbuf_tensor("wo_raw", [P, W_SLOTS, D_MODEL], F32))
        self.ya = c.enter_context(nc.sbuf_tensor("ya", [P, TPG, KB // 2, P], F32))
        self.yb = c.enter_context(nc.sbuf_tensor("yb", [P, SEQ], F32))
        self.loaded = [c.enter_context(nc.semaphore(f"wo_loaded{s}")) for s in range(W_SLOTS)]
        self.ya_in = [c.enter_context(nc.semaphore(f"ya_in{s}")) for s in range(TPG)]
        self.yb_out = [c.enter_context(nc.semaphore(f"yb_out{s}")) for s in range(2)]
        self.view = t["w_out"].rearrange("l (k p) n -> p (l k) n", p=P)
        self.ya_view = t["y"][0:SWA_Q * HD, :].rearrange("(k p) t -> p k t", p=P)


def mix_out(nc, c, t, wo):
    from concourse.bass import ds
    sb = lambda n, s, d=F32: c.enter_context(nc.sbuf_tensor(n, s, d))
    sem = lambda n: c.enter_context(nc.semaphore(n))
    w_hi, w_lo = sb("wo_hi", [P, KB, D_MODEL], F32R), sb("wo_lo", [P, KB, D_MODEL], F32R)
    half = KB // 2
    ya, yb = wo.ya, sb("yb_raw", [P, TPG, half, P])
    y_hi, y_lo = sb("yo_hi", [P, TPG, KB, P], F32R), sb("yo_lo", [P, TPG, KB, P], F32R)
    x_t, out_t = sb("x_t", [P, TPG, D_MODEL]), sb("out_t", [P, TPG, D_MODEL])
    HALVES = D_MODEL // GRP
    Y_AFTER = (0, 2)
    bank = [c.enter_context(nc.psum_tensor(f"obank{n}", [P, GRP], F32)) for n in range(TPG * HALVES)]
    w_hi_done, w_split = sem("wo_hi_done"), sem("wo_split")
    yb_in, x_in, out_out = ([sem(f"{n}{s}") for s in range(TPG)] for n in ("yb_in", "xo_in", "out_out"))
    y_hi_done, y_split = sem("yo_hi_done"), sem("yo_split")
    tile_done, out_done = sem("tile_done"), sem("out_done")
    block = c.enter_context(nc.Block())
    yb_view = t["y"][SWA_Q * HD:, :].rearrange("(k p) t -> p k t", p=P)

    @block.sync
    def _(sp):
        def load_ya(tile, s):
            sp.dma_start(ya[:, s], wo.ya_view[:, :, ds(tile * P, P)]).then_inc(wo.ya_in[s], 16)

        def load_yb(tile, s):
            sp.dma_start(yb[:, s], yb_view[:, :, ds(tile * P, P)]).then_inc(yb_in[s], 16)

        def load_x(tile, s):
            sp.dma_start(x_t[:, s, :], t["x"][0, ds(tile * P, P), :]).then_inc(x_in[s], 16)

        def store(tile, s):
            sp.wait_ge(out_done, HALVES * (tile + TPG + 1))
            sp.dma_start(t["out"][0, ds(tile * P, P), :], out_t[:, s, :]).then_inc(out_out[s], 16)

        for s in range(2):
            sp.wait_ge(wo.yb_out[s], 16 * (TURNS + 1))
        for s in range(TPG):
            load_yb(s, s)
        for k in range(W_SLOTS, KB):
            sp.wait_ge(w_split, k - W_SLOTS + 1)
            sp.dma_start(wo.raw[:, k % W_SLOTS, :], wo.view[:, k, :]).then_inc(wo.loaded[k % W_SLOTS], 16)
        for s in range(TPG):
            load_x(s, s)
        with sp.Fori(0, NG - 1) as g:
            for s in range(TPG):
                sp.wait_ge(y_split, 2 * (TPG * g + s + 1))
                load_ya(TPG * (g + 1) + s, s)
                load_yb(TPG * (g + 1) + s, s)
            for s in range(TPG):
                store(TPG * g + s, s)
                load_x(TPG * (g + 1) + s, s)
        for s in range(TPG):
            store(TPG * (NG - 1) + s, s)
        for s in range(TPG):
            sp.wait_ge(out_out[s], 16 * (NG + 1))

    @block.scalar
    def _(act):
        def w_high(k):
            act.wait_ge(wo.loaded[k % W_SLOTS], 16 * (k // W_SLOTS + 1))
            act.activation(w_hi[:, k, :], wo.raw[:, k % W_SLOTS, :], ACT.Copy).then_inc(w_hi_done, 1)

        def y_high(g, s, part):
            act.wait_ge((wo.ya_in, yb_in)[part][s], 16 * (g + 1))
            act.wait_ge(tile_done, HALVES * (TPG * g + s + 1))
            act.activation(y_hi[:, s, half * part:half * part + half], (ya, yb)[part][:, s],
                           ACT.Copy).then_inc(y_hi_done, 1)

        act.sem_inc(tile_done, HALVES * TPG)
        act.sem_inc(out_done, HALVES * TPG)
        for s in range(TPG):
            act.sem_inc(out_out[s], 16)
        for k in range(KB):
            w_high(k)
            if k in Y_AFTER:
                for s in range(TPG):
                    y_high(0, s, Y_AFTER.index(k))
        with act.Fori(1, NG) as g:
            for s in range(TPG):
                for part in range(2):
                    y_high(g, s, part)

    @block.tensor
    def _(pe):
        passes = ((y_hi, w_hi), (y_hi, w_lo), (y_lo, w_hi))

        def product(s, h, k, n):
            y_part, w_part = passes[n]
            return pe.matmul(bank[HALVES * s + h][:, :], y_part[:, s, k, :], w_part[:, k, h * GRP:(h + 1) * GRP],
                             start=k == 0 and n == 0, stop=k == KB - 1 and n == len(passes) - 1)

        for k in range(KB):
            pe.wait_ge(w_split, k + 1)
            for s in range(TPG):
                if k in (0, half):
                    pe.wait_ge(y_split, TPG * (k // half) + s + 1)
                for h in range(HALVES):
                    for n in range(len(passes)):
                        ins = product(s, h, k, n)
                    if k == KB - 1:
                        ins.then_inc(tile_done, 1)
        with pe.Fori(1, NG) as g:
            for s in range(TPG):
                pe.wait_ge(y_split, 2 * (TPG * g + s + 1))
                for h in range(HALVES):
                    pe.wait_ge(out_done, HALVES * (TPG * g + s) + h + 1)
                    for k in range(KB):
                        for n in range(len(passes)):
                            ins = product(s, h, k, n)
                    ins.then_inc(tile_done, 1)

    @block.vector
    def _(dve):
        def w_low(k):
            dve.wait_ge(w_hi_done, k + 1)
            dve.tensor_tensor(w_lo[:, k, :], wo.raw[:, k % W_SLOTS, :], w_hi[:, k, :].bitcast(F32),
                              ALU.subtract).then_inc(w_split, 1)

        def y_low(s, part, n):
            at = slice(half * part, half * part + half)
            dve.wait_ge(y_hi_done, n + 1)
            dve.tensor_tensor(y_lo[:, s, at], (ya, yb)[part][:, s], y_hi[:, s, at].bitcast(F32),
                              ALU.subtract).then_inc(y_split, 1)

        def add_x(g, s):
            dve.wait_ge(x_in[s], 16 * (g + 1))
            dve.wait_ge(out_out[s], 16 * (g + 1))
            for h in range(HALVES):
                at = slice(h * GRP, (h + 1) * GRP)
                dve.wait_ge(tile_done, HALVES * (TPG * (g + 1) + s) + h + 1)
                dve.tensor_tensor(out_t[:, s, at], bank[HALVES * s + h][:, :], x_t[:, s, at],
                                  ALU.add).then_inc(out_done, 1)

        for k in range(KB):
            w_low(k)
            if k in Y_AFTER:
                part = Y_AFTER.index(k)
                for s in range(TPG):
                    y_low(s, part, TPG * part + s)
        with dve.Fori(0, NG - 1) as g:
            for s in range(TPG):
                add_x(g, s)
                for part in range(2):
                    y_low(s, part, 2 * (TPG * (g + 1) + s) + part)
        for s in range(TPG):
            add_x(NG - 1, s)


def build(nc, t):
    with ExitStack() as c:
        stores = Stores(nc, c)
        with ExitStack() as c1:
            project(nc, c1, t, stores)
        wo = MixInputs(nc, c, t)
        with ExitStack() as c2:
            sticks(nc, c2, t, stores, wo)
        with ExitStack() as c3:
            mix_out(nc, c3, t, wo)


def kernel(**inputs):
    import concourse.bacc as bacc
    from concourse.bass_utils import run_bass_kernel_spmd

    nc = bacc.Bacc("TRN2", target_bir_lowering=False, num_devices=1)
    arrays, t = {}, {}
    for name in ("x", "positions", "norm_gain", "w_in", "q_norm_gain", "k_norm_gain", "sinks", "w_out"):
        a = np.ascontiguousarray(inputs[name])
        arrays[f"in_{name}"] = a
        t[name] = nc.dram_tensor(f"in_{name}", a.shape, mybir.dt.from_np(a.dtype), kind="ExternalInput").ap()
    for name, rows in (("raw", RAW_BLOCKS * P), ("hi", SPLIT_BLOCKS * P), ("lo", SPLIT_BLOCKS * P),
                       ("y", D_MODEL)):
        t[name] = nc.dram_tensor(f"scratch_{name}", (rows, SEQ), F32).ap()
    t["out"] = nc.dram_tensor("out", (1, SEQ, D_MODEL), F32, kind="ExternalOutput").ap()
    build(nc, t)
    r = run_bass_kernel_spmd(nc, [arrays], core_ids=[0])
    return r.results[0]["out"]
```
